# Optimizing a Trainium2 kernel written in Bass

```python
import math
import jax, jax.numpy as jnp
from jax import lax
import numpy as np

D_MODEL = 1024
BATCH = 1
SEQ = 2048
DEPTH = 1

CONV_WIDTH = D_MODEL // 2
CONV_K = 3
HEAD_DIM = 64
N_HEADS = (D_MODEL - CONV_WIDTH) // HEAD_DIM
N_KV_HEADS = 2
GQA_GROUP = N_HEADS // N_KV_HEADS
ATTN_WIDTH = N_HEADS * HEAD_DIM
KV_WIDTH = N_KV_HEADS * HEAD_DIM
WINDOW = 128
BLK = 128
NUM_BUCKETS = 32
MAX_DISTANCE = 128
MAX_EXACT = NUM_BUCKETS // 2
D_FF = 2816
FFN_K = 3
EPS = 1e-6
NEG_INF = -1e30
IN_WIDTH = 3 * CONV_WIDTH + ATTN_WIDTH + 2 * KV_WIDTH

kernel_name = "hybrid_shortconv_swa_sink_convffn"

def rms_norm(x, g):
    xf = x.astype(jnp.float32)
    y = xf * lax.rsqrt(jnp.mean(xf * xf, axis=-1, keepdims=True) + EPS)
    return (y * g.astype(jnp.float32)).astype(x.dtype)

def causal_dwconv(x, w):
    K = w.shape[0]
    S = x.shape[1]
    xp = jnp.pad(x, ((0, 0), (K - 1, 0), (0, 0)))
    y = xp[:, 0:S] * w[0]
    for k in range(1, K):
        y = y + xp[:, k:k + S] * w[k]
    return y

def band_offsets():
    q = jnp.arange(BLK, dtype=jnp.int32)[:, None]
    j = jnp.arange(2 * BLK, dtype=jnp.int32)[None, :]
    return q + BLK - j

def t5_band_bias(rel_table, d):
    n = jnp.maximum(d, 0)
    nf = jnp.maximum(n, 1).astype(jnp.float32)
    large = MAX_EXACT + (jnp.log(nf / MAX_EXACT) / math.log(MAX_DISTANCE / MAX_EXACT)
                         * (NUM_BUCKETS - MAX_EXACT)).astype(jnp.int32)
    large = jnp.minimum(large, NUM_BUCKETS - 1)
    bucket = jnp.where(n < MAX_EXACT, n, large)
    bias = rel_table[bucket].astype(jnp.float32)
    return bias.transpose(2, 0, 1).reshape(N_KV_HEADS, GQA_GROUP, BLK, 2 * BLK)

def band_blocks(t):
    Bn, S = t.shape[0], t.shape[1]
    nb = S // BLK
    tb = t.reshape(Bn, nb, BLK, N_KV_HEADS, HEAD_DIM)
    prev = jnp.pad(tb, ((0, 0), (1, 0), (0, 0), (0, 0), (0, 0)))[:, :-1]
    return jnp.concatenate([prev, tb], axis=2)

def sliding_window_attention(q, k, v, sinks, bias, d):
    Bn, S = q.shape[0], q.shape[1]
    nb = S // BLK
    qb = q.reshape(Bn, nb, BLK, N_KV_HEADS, GQA_GROUP, HEAD_DIM)
    kband = band_blocks(k)
    vband = band_blocks(v)
    scale = HEAD_DIM ** -0.5
    logits = jnp.einsum('bnqhgd,bnkhd->bnhgqk', qb, kband).astype(jnp.float32) * scale + bias
    within = (d >= 0) & (d < WINDOW)
    key_pos = (jnp.arange(nb, dtype=jnp.int32)[:, None, None] - 1) * BLK \
        + jnp.arange(2 * BLK, dtype=jnp.int32)[None, None, :]
    valid = within[None] & (key_pos >= 0)
    logits = jnp.where(valid[None, :, None, None], logits, NEG_INF)
    sink = sinks.astype(jnp.float32).reshape(1, 1, N_KV_HEADS, GQA_GROUP, 1, 1)
    m = jnp.maximum(jnp.max(logits, axis=-1, keepdims=True), sink)
    p = jnp.exp(logits - m)
    denom = jnp.sum(p, axis=-1, keepdims=True) + jnp.exp(sink - m)
    probs = (p / denom).astype(v.dtype)
    out = jnp.einsum('bnhgqk,bnkhd->bnqhgd', probs, vband)
    return out.reshape(Bn, S, ATTN_WIDTH)

def setup_inputs(seed: int = 0) -> dict:
    key = jax.random.key(seed)
    ks = jax.random.split(key, 17)
    f32 = jnp.float32

    def nrm(k, shape, scale):
        return jax.random.normal(k, shape, f32) * scale

    def gain(k, shape):
        return 1.0 + 0.02 * jax.random.normal(k, shape, f32)

    return {
        "x": jax.random.normal(ks[0], (BATCH, SEQ, D_MODEL), f32),
        "norm_mix_g": gain(ks[1], (DEPTH, D_MODEL)),
        "w_in": nrm(ks[2], (DEPTH, D_MODEL, IN_WIDTH), D_MODEL ** -0.5),
        "conv_w": nrm(ks[3], (DEPTH, CONV_K, CONV_WIDTH), CONV_K ** -0.5),
        "q_norm_g": gain(ks[4], (DEPTH, HEAD_DIM)),
        "k_norm_g": gain(ks[5], (DEPTH, HEAD_DIM)),
        "rel_bias_table": nrm(ks[6], (NUM_BUCKETS, N_HEADS), 0.5),
        "sinks": nrm(ks[7], (DEPTH, N_HEADS), 1.0),
        "out_norm_conv_g": gain(ks[8], (DEPTH, CONV_WIDTH)),
        "out_norm_attn_g": gain(ks[9], (DEPTH, ATTN_WIDTH)),
        "w_out": nrm(ks[10], (DEPTH, CONV_WIDTH + ATTN_WIDTH, D_MODEL), (CONV_WIDTH + ATTN_WIDTH) ** -0.5),
        "norm_ffn_g": gain(ks[11], (DEPTH, D_MODEL)),
        "w_up": nrm(ks[12], (DEPTH, D_MODEL, 2 * D_FF), D_MODEL ** -0.5),
        "ffn_conv_w": nrm(ks[13], (DEPTH, FFN_K, 2 * D_FF), FFN_K ** -0.5),
        "ffn_conv_b": nrm(ks[14], (DEPTH, 2 * D_FF), 0.02),
        "w_down": nrm(ks[15], (DEPTH, D_FF, D_MODEL), D_FF ** -0.5),
    }

def reference(x, norm_mix_g, w_in, conv_w, q_norm_g, k_norm_g, rel_bias_table, sinks,
              out_norm_conv_g, out_norm_attn_g, w_out, norm_ffn_g, w_up, ffn_conv_w,
              ffn_conv_b, w_down):
    Bn, S, _ = x.shape
    d = band_offsets()
    bias = t5_band_bias(rel_bias_table, d)
    h = x
    for l in range(DEPTH):
        u = rms_norm(h, norm_mix_g[l])
        proj = jnp.einsum('bsd,de->bse', u, w_in[l])
        c0 = 0
        gate_b = proj[..., c0:c0 + CONV_WIDTH]; c0 += CONV_WIDTH
        gate_c = proj[..., c0:c0 + CONV_WIDTH]; c0 += CONV_WIDTH
        hc = proj[..., c0:c0 + CONV_WIDTH]; c0 += CONV_WIDTH
        q = proj[..., c0:c0 + ATTN_WIDTH]; c0 += ATTN_WIDTH
        k = proj[..., c0:c0 + KV_WIDTH]; c0 += KV_WIDTH
        v = proj[..., c0:c0 + KV_WIDTH]

        y_conv = gate_b * causal_dwconv(gate_c * hc, conv_w[l])

        q = rms_norm(q.reshape(Bn, S, N_HEADS, HEAD_DIM), q_norm_g[l])
        k = rms_norm(k.reshape(Bn, S, N_KV_HEADS, HEAD_DIM), k_norm_g[l])
        v = v.reshape(Bn, S, N_KV_HEADS, HEAD_DIM)
        y_attn = sliding_window_attention(q, k, v, sinks[l], bias, d)

        y = jnp.concatenate([rms_norm(y_conv, out_norm_conv_g[l]),
                             rms_norm(y_attn, out_norm_attn_g[l])], axis=-1)
        h = h + jnp.einsum('bse,ed->bsd', y, w_out[l])

        u = rms_norm(h, norm_ffn_g[l])
        up = jnp.einsum('bsd,df->bsf', u, w_up[l])
        up = causal_dwconv(up, ffn_conv_w[l]) + ffn_conv_b[l]
        g, val = up[..., :D_FF], up[..., D_FF:]
        h = h + jnp.einsum('bsf,fd->bsd', jax.nn.silu(g) * val, w_down[l])
    return h


_drawn_inputs = setup_inputs


def setup_inputs(seed=0):
    import zlib

    import numpy as np

    out = dict(_drawn_inputs(seed))
    spreads = {}
    factors = {'q_norm_g': 5.825,
     'k_norm_g': 4.992,
     'sinks': 181.303,
     'out_norm_conv_g': 56.372,
     'out_norm_attn_g': 54.425,
     'norm_ffn_g': 13.514,
     'ffn_conv_b': 13.788}
    for name, (base, spread) in spreads.items():
        noise = np.random.default_rng([zlib.crc32(name.encode()), seed]).standard_normal(out[name].shape)
        drawn = base * np.exp(spread * noise) if base else spread * noise
        out[name] = __import__('jax').numpy.asarray(drawn.astype(out[name].dtype))
    for name, factor in factors.items():
        out[name] = (out[name] * factor).astype(out[name].dtype)
    return out
```

```python
import math
from contextlib import ExitStack

import numpy as np

import concourse.bass as bass
from concourse import mybir

F32 = mybir.dt.float32
F32R = mybir.dt.float32r
ACT = mybir.ActivationFunctionType
ALU = mybir.AluOpType
AXIS_X = mybir.AxisListType.X

P = 128
D_MODEL, SEQ = 1024, 2048
CONV_WIDTH, ATTN_WIDTH, HEAD_DIM, N_HEADS, N_KV = 512, 512, 64, 8, 2
KV_WIDTH = N_KV * HEAD_DIM
D_FF = 2816
NUM_BUCKETS, MAX_DISTANCE, WINDOW = 32, 128, 128
MAX_EXACT = NUM_BUCKETS // 2
EPS = 1e-6
MASKED = -1e30

T = 512
CHUNKS = SEQ // T
KD = D_MODEL // P
QT = N_HEADS // 2
CT = CONV_WIDTH // P
BLOCKS = T // P
HALVES = 2 * BLOCKS
FT = D_FF // P
PART_A, PART_B = 12, 10
SLOTS = 4
RAW_SLOTS = 2

U_K, U_V, U_Q, U_CONV = 0, 1, 2, 2 + QT
U_OUT = U_CONV + 3 * CT
U_UP_A = U_OUT + KD
U_DOWN_A = U_UP_A + 2 * PART_A
U_UP_B = U_DOWN_A + PART_A * KD // 8
U_DOWN_B = U_UP_B + 2 * PART_B
UNITS = U_DOWN_B + PART_B * KD // 8

T_OUT = U_OUT
T_UP_A = T_OUT + KD
T_DOWN_A = T_UP_A + 2 * PART_A
T_UP_B = T_DOWN_A + KD
T_DOWN_B = T_UP_B + 2 * PART_B
TILES = T_DOWN_B + KD

DOWN_ENDS = {n: sorted({k for k in range(1, n * KD + 1) if k % 8 == 0 or k % n == 0}) for n in (PART_A, PART_B)}
E_DOWN_A = U_DOWN_A
E_UP_B = E_DOWN_A + len(DOWN_ENDS[PART_A])
E_DOWN_B = E_UP_B + 2 * PART_B
EVENTS = E_DOWN_B + len(DOWN_ENDS[PART_B])


def unit_end(u):
    for unit0, event0, part in ((U_DOWN_B, E_DOWN_B, PART_B), (U_DOWN_A, E_DOWN_A, PART_A)):
        if unit0 <= u < unit0 + part * KD // 8:
            return event0 + DOWN_ENDS[part].index(8 * (u - unit0 + 1)) + 1
    return (u + 1) if u < U_DOWN_A else E_UP_B + (u - U_UP_B) + 1


def tile_end(t):
    for tile0, event0, part in ((T_DOWN_B, E_DOWN_B, PART_B), (T_DOWN_A, E_DOWN_A, PART_A)):
        if tile0 <= t < tile0 + KD:
            return event0 + DOWN_ENDS[part].index(part * (t - tile0 + 1)) + 1
    return (t + 1) if t < T_DOWN_A else E_UP_B + (t - T_UP_B) + 1


ST_MIX, ST_K, ST_Q, ST_CONV, ST_ATTN, ST_FFN = 0, 1, 2, 2 + QT, 3 + QT, 4 + QT
STATS = 5 + QT
N_MIX, N_K, N_Q = 0, KD, KD + 1
N_CONV = N_Q + QT
N_ATTN = N_CONV + CT
N_FFN = N_ATTN + QT
NORMED = N_FFN + KD
Q_MIX, Q_CONV = 0, KD
Q_ATTN = Q_CONV + CT
Q_FFN = Q_ATTN + QT
SQUARES = Q_FFN + KD

V_MIX_G, V_FFN_G = 0, KD
V_CONV_G = 2 * KD
V_ATTN_G = V_CONV_G + CT
V_Q_G = V_ATTN_G + QT
V_K_G = V_Q_G + 1
V_CONV_W = V_K_G + 1
V_SINKS = V_CONV_W + 3 * CT
V_FFN = V_SINKS + N_HEADS
V_COLS = V_FFN + FT * 2 * 4
REL = 3 * P


def build_layer(nc, x, weights, vectors, rel_table, fixed, bucket_rows, bias_rows, out):
    ctx = ExitStack()
    with ctx:
        def sb(name, shape, dt=F32):
            return ctx.enter_context(nc.sbuf_tensor(name, shape, dt))

        def sem(name):
            return ctx.enter_context(nc.semaphore(name))

        w_raw = sb("w_raw", [P, RAW_SLOTS, KD * P])
        w_hi = sb("w_hi", [P, SLOTS, KD * P], F32R)
        w_lo = sb("w_lo", [P, SLOTS, KD * P], F32R)
        x_in = sb("x_in", [P, KD, T])
        h = sb("h", [P, KD, T])
        u_hi = sb("u_hi", [P, KD, T], F32R)
        u_lo = sb("u_lo", [P, KD, T], F32R)
        g_hi = sb("g_hi", [P, PART_A, T], F32R)
        g_lo = sb("g_lo", [P, PART_A, T], F32R)
        k_hi = sb("k_hi", [P, P + T], F32R)
        k_lo = sb("k_lo", [P, P + T], F32R)
        v_sb = sb("v_sb", [P, 1 + BLOCKS, P])
        gated = sb("gated", [P, CT, 2 + T])
        up_tail = sb("up_tail", [P, FT, 2, 2])
        square = sb("square", [P, 2, T])
        square_sum = sb("square_sum", [P, T])
        rstd = sb("rstd", [P, T])
        normed = sb("normed", [P, 2, T])
        shared = sb("shared", [P, 7 * T])
        scores = shared[:, 0:2 * T].rearrange("p (n k) -> p n k", n=4)
        probs_t = shared[:, 2 * T:4 * T].rearrange("p (n k) -> p n k", n=2)
        gate_c = shared[:, 4 * T:5 * T]
        conv = shared[:, 5 * T:6 * T]
        heads = shared[:, 6 * T:7 * T]
        v_t = conv
        up_conv = shared[:, 0:2 * T].rearrange("p (n t) -> p n t", n=2)
        product32 = shared[:, 2 * T:3 * T]
        up = shared[:, 3 * T:5 * T + 4].rearrange("p (n t) -> p n t", n=2)
        bias = sb("bias", [P, N_HEADS, 2 * P])
        vec = sb("vec", [P, V_COLS])
        table = sb("table", [NUM_BUCKETS + 1, N_HEADS])
        fix = sb("fix", [P, 2, P])
        mean_model = sb("mean_model", [P, P])[:, :]
        mean_branch = sb("mean_branch", [P, P])[:, :]
        edge = sb("edge", [P, 1])
        eps = sb("eps", [P, 1])
        top = sb("top", [P, N_HEADS])
        neg_top = sb("neg_top", [P, N_HEADS])
        sink_less = sb("sink_less", [P, N_HEADS])
        sink_exp = sb("sink_exp", [P, 2, N_HEADS])
        denom = sb("denom", [P, 2, N_HEADS])
        identity, mean_head = fix[:, 0, :], fix[:, 1, :]
        table_wide = shared[0:NUM_BUCKETS + 1, 0:N_HEADS * P].rearrange("p (n k) -> p n k", n=N_HEADS)
        buckets = shared[0:NUM_BUCKETS + 1, 2 * T:2 * T + REL]
        row = shared[:, 3 * T:3 * T + 2 * REL].rearrange("p (n k) -> p n k", n=2)

        psum = ctx.enter_context(nc.psum_tensor("psum", [P, 8, T], F32))
        S_BANK, PT_BANKS, STAT_BANK = 4, (6, 3), 7

        w_loaded = [sem(f"w_loaded{s}") for s in range(RAW_SLOTS)]
        w_hi_done, w_ready = sem("w_hi_done"), sem("w_ready")
        pe_done = sem("pe_done")
        bank_free = [sem(f"bank_free{b}") for b in range(4)]
        stat_done, std_ready = sem("stat_done"), sem("std_ready")
        qk_square = sem("qk_square")
        square_ready, square_added = sem("square_ready"), sem("square_added")
        normed_ready, hi_done, lo_done = sem("normed_ready"), sem("hi_done"), sem("lo_done")
        v_copied, v_turned, v_ready, tails_moved = sem("v_copied"), sem("v_turned"), sem("v_ready"), sem("tails_moved")
        scores_done, top_ready, exp_done = sem("scores_done"), sem("top_ready"), sem("exp_done")
        turned, pt_first, pt_second = sem("turned"), sem("pt_first"), sem("pt_second")
        pv_done, heads_ready = sem("pv_done"), sem("heads_ready")
        heads_turned, heads_stored = sem("heads_turned"), sem("heads_stored")
        c_copied, gated_ready, tap_done, y_ready = sem("c_copied"), sem("gated_ready"), sem("tap_done"), sem("y_ready")
        h_ready = sem("h_ready")
        up_copied, conv_done, silu_done = sem("up_copied"), sem("conv_done"), sem("silu_done")
        product_ready, g_hi_done, g_ready = sem("product_ready"), sem("g_hi_done"), sem("g_ready")
        x_loaded, x_used, out_ready, out_stored = sem("x_loaded"), sem("x_used"), sem("out_ready"), sem("out_stored")
        consts, vec_loaded = sem("consts"), sem("vec_loaded")
        wide_ready, row_done, row_copied = sem("wide_ready"), sem("row_done"), sem("row_copied")
        row_stored, bias_loaded = [sem("row_stored0"), sem("row_stored1")], sem("bias_loaded")

        def bank_of(tile):
            if tile < T_OUT:
                return tile % 3
            for first in (T_DOWN_B, T_UP_B, T_DOWN_A, T_UP_A, T_OUT):
                if tile >= first:
                    return (tile - first) % 4

        USES = [sum(bank_of(t) == b for t in range(TILES)) for b in range(4)]

        def uses_before(tile):
            return sum(bank_of(t) == bank_of(tile) for t in range(tile))

        block = ctx.enter_context(nc.Block())

        @block.sync
        def _(sp):
            def load(unit, slot):
                sp.dma_start(w_raw[:, slot, :], weights[bass.ds(unit, 1), :, :].rearrange("a p n -> p (a n)")) \
                  .then_inc(w_loaded[slot], 16)

            for s in range(RAW_SLOTS):
                load(s, s)
            with sp.Fori(1, UNITS // RAW_SLOTS) as i:
                for s in range(RAW_SLOTS):
                    unit = sp.snap(i * RAW_SLOTS + s)
                    sp.wait_ge(w_ready, i * RAW_SLOTS + (s + 1 - RAW_SLOTS))
                    load(unit, s)
            with sp.Fori(1, CHUNKS) as c:
                with sp.Fori(0, UNITS // RAW_SLOTS) as i:
                    for s in range(RAW_SLOTS):
                        unit = sp.snap(i * RAW_SLOTS + s)
                        sp.wait_ge(w_ready, c * UNITS + i * RAW_SLOTS + (s + 1 - RAW_SLOTS))
                        load(unit, s)

        @block.gpsimd
        def _(pool):
            with pool.Fori(0, CHUNKS * UNITS // SLOTS) as i:
                for s in range(SLOTS):
                    pool.wait_ge(w_hi_done, i * SLOTS + (s + 1))
                    pool.tensor_tensor(w_lo[:, s, :], w_raw[:, s % RAW_SLOTS, :], w_hi[:, s, :].bitcast(F32),
                                       ALU.subtract).then_inc(w_ready, 1)

        @block.tensor
        def _(pe):
            def product(c, tile, bank, free, pairs, middle=None):
                pe.wait_ge(bank_free[bank], free)
                seen = None
                for n, (unit, name, k, last_use, a_hi, a_lo, waits) in enumerate(pairs):
                    if name != seen:
                        pe.wait_ge(w_ready, unit + 1)
                        seen = name
                    for s, v in waits:
                        pe.wait_ge(s, v)
                    slot = name % SLOTS
                    hi, lo = w_hi[:, slot, k * P:(k + 1) * P], w_lo[:, slot, k * P:(k + 1) * P]
                    end = n == len(pairs) - 1
                    pe.matmul(psum[:, bank, :], hi, a_hi, start=n == 0, stop=False)
                    pe.matmul(psum[:, bank, :], hi, a_lo, start=False, stop=False)
                    mm = pe.matmul(psum[:, bank, :], lo, a_hi, start=False, stop=end)
                    if last_use or end:
                        mm.then_inc(pe_done, 1)
                    if middle and n == len(pairs) // 2 - 1:
                        middle()

            def projection(c, tile, unit, name, a_hi, a_lo, first=None, middle=None, free=None, bank=None):
                pairs = [(unit, name, k, k == KD - 1, a_hi[:, k, :], a_lo[:, k, :],
                          [(lo_done, first + k + 1)] if first is not None else []) for k in range(KD)]
                bank = bank_of(tile) if bank is None else bank
                free = c * USES[bank] + (uses_before(tile) + 1) if free is None else free
                product(c, tile, bank, free, pairs, middle)

            def statistic(c, index, ready, value, mean, squares):
                pe.wait_ge(ready, value)
                if not (isinstance(c, int) and c == 0 and index == 0):
                    pe.wait_ge(std_ready, c * STATS + index)
                pe.matmul(psum[:, STAT_BANK, :], mean, squares, start=True, stop=True).then_inc(stat_done, 1)

            def qk_statistic(c, n):
                statistic(c, ST_K + n, qk_square, c * (1 + QT) + (n + 1), mean_head, square[:, 0, :])

            def turn_v(c):
                pe.wait_ge(v_copied, c + 1)
                for b in range(BLOCKS):
                    mm = pe.transpose(psum[:, PT_BANKS[0], b * P:(b + 1) * P], v_t[:, b * P:(b + 1) * P], identity)
                mm.then_inc(v_turned, 1)

            def score(c, m):
                i, hf = m // 2, m % 2
                if m == 0:
                    pe.wait_ge(lo_done, c * NORMED + N_CONV)
                for n in range(2):
                    p = 2 * hf + n
                    for e in range(2):
                        rows = slice(e * HEAD_DIM, (e + 1) * HEAD_DIM)
                        o = psum[:, S_BANK + e, n * 2 * P:(n + 1) * 2 * P]
                        qh, ql = (g[rows, KD + p, i * P:(i + 1) * P] for g in (g_hi, g_lo))
                        kh, kl = (k[rows, i * P:(i + 2) * P] for k in (k_hi, k_lo))
                        pe.matmul(o, qh, kh, start=True, stop=False)
                        pe.matmul(o, qh, kl, start=False, stop=False)
                        mm = pe.matmul(o, ql, kh, start=False, stop=True)
                mm.then_inc(scores_done, 1)

            def turn_probs(c, m):
                pe.wait_ge(exp_done, c * HALVES + (m + 1))
                if m == 0:
                    pe.wait_ge(v_ready, c + 1)
                    pe.wait_ge(bank_free[3], c * USES[3] + 1)
                if m % 2 == 1 and m >= 3:
                    pe.wait_ge(heads_stored, c * BLOCKS + (m - 1) // 2)
                for e in range(2):
                    for n in range(2):
                        for kt in range(2):
                            at = 2 * n + kt
                            mm = pe.transpose(psum[:, PT_BANKS[e], at * P:(at + 1) * P],
                                              scores[:, 2 * e + n, kt * P:(kt + 1) * P], identity)
                    mm.then_inc(turned, 1)

            def weigh_values(c, m):
                i, hf = m // 2, m % 2
                pe.wait_ge(pt_first, c * HALVES + (m + 1))
                pe.wait_ge(pt_second, c * HALVES + (m + 1))
                if m == 0:
                    pe.wait_ge(std_ready, c * STATS + ST_CONV)
                elif hf == 0:
                    pe.wait_ge(heads_ready, c * BLOCKS + i)
                for e in range(2):
                    for n in range(2):
                        at = (4 * hf + 2 * e + n) * HEAD_DIM
                        for kt in range(2):
                            mm = pe.matmul(psum[:, STAT_BANK, at:at + HEAD_DIM],
                                           probs_t[:, e, (2 * n + kt) * P:(2 * n + kt + 1) * P],
                                           v_sb[:, i + kt, e * HEAD_DIM:(e + 1) * HEAD_DIM],
                                           start=kt == 0, stop=kt == 1)
                mm.then_inc(pv_done, 1)

            def turn_heads(c, i):
                pe.wait_ge(heads_ready, c * BLOCKS + (i + 1))
                pe.wait_ge(pt_first, c * HALVES + min(2 * i + 3, HALVES))
                for p in range(QT):
                    mm = pe.transpose(psum[:, PT_BANKS[0], p * P:(p + 1) * P], heads[:, p * P:(p + 1) * P], identity)
                mm.then_inc(heads_turned, 1)

            def attention_step(c, m):
                if m >= 4 and m % 2 == 0:
                    turn_heads(c, m // 2 - 2)
                if 2 <= m < HALVES + 2:
                    weigh_values(c, m - 2)
                if 1 <= m < HALVES + 1:
                    turn_probs(c, m - 1)
                if m < HALVES:
                    score(c, m)

            def up_projection(c, tile0, unit0, part, first=None):
                with pe.Fori(0, part // 2) as i:
                    for n in range(4):
                        projection(c, tile0 + n, c * UNITS + i * 4 + (unit0 + n), unit0 + n, u_hi, u_lo,
                                   first=first if n == 0 else None,
                                   free=c * USES[n] + i + (uses_before(tile0 + n) + 1), bank=n)

            def down_projection(c, tile0, unit0, part, g0, middle=None):
                for d in range(KD):
                    pairs = []
                    for k in range(part):
                        at = d * part + k
                        pairs.append((c * UNITS + (unit0 + at // 8), unit0 + at // 8, at % 8,
                                      at % 8 == 7, g_hi[:, k, :], g_lo[:, k, :],
                                      [(g_ready, c * FT + (g0 + k + 1))] if d == 0 else []))
                    product(c, tile0 + d, bank_of(tile0 + d),
                            c * USES[bank_of(tile0 + d)] + (uses_before(tile0 + d) + 1), pairs,
                            middle if d == 3 else None)

            def chunk(c, last):
                def unit(n):
                    return c * UNITS + n

                projection(c, U_K, unit(U_K), U_K, u_hi, u_lo, first=c * NORMED + N_MIX)
                projection(c, U_V, unit(U_V), U_V, u_hi, u_lo, middle=lambda: qk_statistic(c, 0))
                projection(c, U_Q, unit(U_Q), U_Q, u_hi, u_lo, middle=lambda: turn_v(c))
                for p in range(1, QT):
                    projection(c, U_Q + p, unit(U_Q + p), U_Q + p, u_hi, u_lo,
                               middle=lambda p=p: qk_statistic(c, p))
                projection(c, U_CONV, unit(U_CONV), U_CONV, u_hi, u_lo, middle=lambda: qk_statistic(c, QT))
                for m in range(3 * CT - 1):
                    projection(c, U_CONV + 1 + m, unit(U_CONV + 1 + m), U_CONV + 1 + m, u_hi, u_lo)
                    attention_step(c, m)
                statistic(c, ST_CONV, square_added, c * SQUARES + Q_ATTN, mean_branch, square_sum[:, :])
                statistic(c, ST_ATTN, square_added, c * SQUARES + Q_FFN, mean_branch, square_sum[:, :])
                for d in range(KD):
                    projection(c, T_OUT + d, unit(U_OUT + d), U_OUT + d, g_hi, g_lo,
                               first=c * NORMED + N_CONV if d == 0 else None)
                statistic(c, ST_FFN, square_added, c * SQUARES + SQUARES, mean_model, square_sum[:, :])
                up_projection(c, T_UP_A, U_UP_A, PART_A, first=c * NORMED + N_FFN)
                down_projection(c, T_DOWN_A, U_DOWN_A, PART_A, 0)
                up_projection(c, T_UP_B, U_UP_B, PART_B)
                nxt = c + 1
                down_projection(c, T_DOWN_B, U_DOWN_B, PART_B, PART_A,
                                None if last else lambda: statistic(nxt, ST_MIX, square_added,
                                                                    nxt * SQUARES + Q_CONV, mean_model,
                                                                    square_sum[:, :]))

            pe.wait_ge(consts, 2)
            pe.wait_ge(vec_loaded, 64)
            pe.wait_ge(wide_ready, 1)
            for n in range(N_HEADS):
                if n >= 2:
                    pe.wait_ge(row_copied, n - 1)
                pe.matmul(psum[:, n % 2, 0:REL], table_wide[:, n, :], buckets, start=True, stop=True).then_inc(row_done, 1)
            pe.wait_ge(row_copied, N_HEADS)
            statistic(0, ST_MIX, square_added, Q_CONV, mean_model, square_sum[:, :])
            with pe.Fori(0, CHUNKS - 1) as c:
                chunk(c, False)
            chunk(CHUNKS - 1, True)

        @block.scalar
        def _(act):
            state = [0]

            def split_to(c, n):
                while state[0] < n:
                    u = state[0]
                    before = unit_end(u - SLOTS) if u >= SLOTS else unit_end(u - SLOTS + UNITS) - EVENTS
                    split_one(u, c * (UNITS // RAW_SLOTS) * 16 + 16 * (u // RAW_SLOTS + 1),
                              c * EVENTS + (before + 1))
                    state[0] += 1

            def split_one(name, loads, used):
                slot, raw = name % SLOTS, name % RAW_SLOTS
                act.wait_ge(w_loaded[raw], loads)
                if used is not None:
                    act.wait_ge(pe_done, used)
                act.activation(w_hi[:, slot, :], w_raw[:, raw, :], ACT.Copy).then_inc(w_hi_done, 1)

            def square_tiles(c, first, tiles, ready=None):
                for n, tile in enumerate(tiles):
                    if ready:
                        act.wait_ge(ready[0], ready[1] + (n + 1))
                    if not (isinstance(c, int) and c == 0 and first + n < 2):
                        act.wait_ge(square_added, c * SQUARES + (first + n - 1))
                    act.activation(square[:, n % 2, :], tile, ACT.Square).then_inc(square_ready, 1)

            def deviation(c, index, used):
                act.wait_ge(stat_done, c * STATS + (index + 1))
                if used is not None:
                    act.wait_ge(normed_ready, used)
                act.activation(rstd[:, :], psum[:, STAT_BANK, :], ACT.Sqrt, bias=eps[:, :]).then_inc(std_ready, 1)

            def round_tile(c, n, target):
                act.wait_ge(normed_ready, c * NORMED + (n + 1))
                act.activation(target, normed[:, n % 2, :], ACT.Copy).then_inc(hi_done, 1)

            def done(c, tile):
                act.wait_ge(pe_done, c * EVENTS + (tile_end(tile) + 1))

            def load_x(c):
                act.dma_start(x_in[:, :, :], x[bass.ds(c, 1), :, :].rearrange("a p (k t) -> p (a k) t", k=KD)) \
                   .then_inc(x_loaded, 16)

            def norm_mix(c):
                act.wait_ge(x_loaded, c * 16 + 16)
                square_tiles(c, Q_MIX, [x_in[:, k, :] for k in range(KD)])
                deviation(c, ST_MIX, None if isinstance(c, int) and c == 0 else c * NORMED)
                for k in range(KD):
                    round_tile(c, N_MIX + k, u_hi[:, k, :])

            def qk_square_of(c, n, tile):
                done(c, tile)
                act.activation(square[:, 0, :], psum[:, bank_of(tile), :], ACT.Square).then_inc(qk_square, 1)

            def exps(c, m):
                hf = m % 2
                act.wait_ge(top_ready, c * HALVES + (m + 1))
                for n in range(4):
                    at = 4 * hf + n
                    act.activation(scores[:, n, :], scores[:, n, :], ACT.Exp, bias=neg_top[:, at:at + 1],
                                   accum_out=denom[:, m // 2 % 2, at:at + 1])
                act.activation(sink_exp[:, m // 2 % 2, 4 * hf:4 * hf + 4], sink_less[:, 4 * hf:4 * hf + 4], ACT.Exp) \
                   .then_inc(exp_done, 1)

            def attention_step(c, m):
                if m >= 4 and m % 2 == 0:
                    i = m // 2 - 2
                    act.wait_ge(heads_turned, c * BLOCKS + (i + 1))
                    act.activation(h[:, CT:KD, i * P:(i + 1) * P],
                                   psum[:, PT_BANKS[0], :].rearrange("p (n t) -> p n t", n=QT), ACT.Copy) \
                       .then_inc(heads_stored, 1)
                if 1 <= m < HALVES + 1:
                    act.wait_ge(turned, c * 2 * HALVES + 2 * m)
                    act.activation(probs_t[:, 1, :], psum[:, PT_BANKS[1], :], ACT.Copy).then_inc(pt_second, 1)
                if m < HALVES:
                    exps(c, m)

            def conv_step(c, n):
                j, kind = n // 3, n % 3
                if kind == 0:
                    done(c, U_CONV + n)
                    if j >= 1:
                        act.wait_ge(gated_ready, c * CT + j)
                    act.activation(gate_c, psum[:, bank_of(U_CONV + n), :], ACT.Copy).then_inc(c_copied, 1)
                if kind == 1:
                    act.wait_ge(gated_ready, c * CT + (j + 1))
                    if j >= 1:
                        act.wait_ge(y_ready, c * CT + j)
                    w = V_CONV_W + 3 * j + 2
                    act.activation(conv, gated[:, j, 2:2 + T], ACT.Copy, scale=vec[:, w:w + 1]).then_inc(tap_done, 1)

            def up_phase(c, tile0, unit0, part, f0):
                with act.Fori(0, part // 2) as i:
                    for e in range(2):
                        f = i * 2 + (f0 + e)
                        pair = c * FT + f
                        for gv in range(2):
                            n = 2 * e + gv
                            split_one(unit0 + n + 3, c * (UNITS // RAW_SLOTS * 16) + i * (4 // RAW_SLOTS * 16)
                                      + ((unit0 + n + 3) // RAW_SLOTS + 1) * 16,
                                      c * EVENTS + i * 4 + (tile_end(tile0 + n)))
                            act.wait_ge(pe_done, c * EVENTS + i * 4 + (tile_end(tile0 + n) + 1))
                            col = V_FFN + gv * 4
                            w2 = vec[:, bass.ds(f * 8 + (col + 2), 1)]
                            b = vec[:, bass.ds(f * 8 + (col + 3), 1)]
                            if gv == 0:
                                act.wait_ge(product_ready, pair + 1)
                            act.activation(up[:, gv, 2:2 + T], psum[:, n, :], ACT.Copy)
                            act.activation(up_conv[:, gv, :], psum[:, n, :], ACT.Identity, scale=w2, bias=b) \
                               .then_inc(up_copied, 1)
                        act.wait_ge(conv_done, pair + 1)
                        act.activation(up_conv[:, 0, :], up_conv[:, 0, :], ACT.Silu).then_inc(silu_done, 1)
                        act.wait_ge(product_ready, pair + 2)
                        act.activation(g_hi[:, bass.ds(i * 2 + e, 1), :].rearrange("p a t -> p (a t)"),
                                       product32, ACT.Copy).then_inc(g_hi_done, 1)
                state[0] += 2 * part

            def chunk(c, last):
                state[0] = 3
                split_to(c, 4)
                qk_square_of(c, 0, U_K)
                split_to(c, 5)
                done(c, U_V)
                act.wait_ge(tails_moved, c + 1)
                act.activation(v_t, psum[:, bank_of(U_V), :], ACT.Copy).then_inc(v_copied, 1)
                deviation(c, ST_K, c * NORMED + N_K)
                round_tile(c, N_K, k_hi[:, P:P + T])
                split_to(c, 6)
                qk_square_of(c, 1, U_Q)
                act.wait_ge(v_turned, c + 1)
                act.activation(v_sb[:, 1:1 + BLOCKS, :],
                               psum[:, PT_BANKS[0], :].rearrange("p (b d) -> p b d", b=BLOCKS), ACT.Copy) \
                   .then_inc(v_ready, 1)
                for p in range(QT):
                    split_to(c, 7 + p)
                    deviation(c, ST_Q + p, c * NORMED + N_Q + p)
                    round_tile(c, N_Q + p, g_hi[:, KD + p, :])
                    if p + 1 < QT:
                        qk_square_of(c, 2 + p, U_Q + p + 1)
                conv_step(c, 0)
                for m in range(3 * CT - 1):
                    split_to(c, U_CONV + 1 + m + 4)
                    conv_step(c, 1 + m)
                    attention_step(c, m)
                    if (1 + m) % 3 == 2:
                        j = (1 + m) // 3
                        square_tiles_at(c, Q_CONV + j, h[:, j, :], y_ready, c * CT + (j + 1))
                deviation(c, ST_CONV, c * NORMED + N_CONV)
                act.wait_ge(stat_done, c * STATS + (ST_CONV + 1))
                for p in range(QT):
                    square_tiles_at(c, Q_ATTN + p, h[:, CT + p, :])
                for j in range(CT):
                    round_tile(c, N_CONV + j, g_hi[:, j, :])
                deviation(c, ST_ATTN, c * NORMED + N_ATTN)
                for p in range(QT):
                    round_tile(c, N_ATTN + p, g_hi[:, CT + p, :])
                for d in range(KD):
                    split_to(c, U_OUT + d + 4)
                    square_tiles_at(c, Q_FFN + d, h[:, d, :], h_ready, c * KD + (d + 1))
                if not last:
                    act.wait_ge(x_used, c + 1)
                    load_x(c + 1)
                deviation(c, ST_FFN, c * NORMED + N_FFN)
                for k in range(KD):
                    round_tile(c, N_FFN + k, u_hi[:, k, :])
                up_phase(c, T_UP_A, U_UP_A, PART_A, 0)
                for d in range(KD):
                    split_to(c, U_DOWN_A + (d * PART_A) // 8 + 4)
                    done(c, T_DOWN_A + d)
                split_to(c, U_UP_B + 3)
                up_phase(c, T_UP_B, U_UP_B, PART_B, PART_A)
                split_to(c, U_DOWN_B + 3)
                if not last:
                    norm_mix_with_splits(c)
                for d in range(KD):
                    split_to(c, min(U_DOWN_B + (d * PART_B) // 8 + 4, UNITS if last else UNITS + 3))
                    if d % 4 == 3:
                        act.wait_ge(out_ready, c * KD + (d + 1))
                        lo = d - 3
                        act.dma_start(out[bass.ds(c, 1), :, lo * T:(lo + 4) * T].rearrange("a p n -> p (a n)"),
                                      h[:, lo:lo + 4, :].rearrange("p k t -> p (k t)")).then_inc(out_stored, 16)
                if not last:
                    split_to(c, UNITS + 3)

            def square_tiles_at(c, n, tile, ready=None, value=None):
                if ready is not None:
                    act.wait_ge(ready, value)
                act.wait_ge(square_added, c * SQUARES + (n - 1))
                act.activation(square[:, n % 2, :], tile, ACT.Square).then_inc(square_ready, 1)

            def norm_mix_with_splits(c):
                nxt = c + 1
                act.wait_ge(x_loaded, nxt * 16 + 16)
                for k in range(KD):
                    square_tiles_at(nxt, Q_MIX + k, x_in[:, k, :])
                split_to(c, U_DOWN_B + 6)
                deviation(nxt, ST_MIX, nxt * NORMED)
                for k in range(KD):
                    round_tile(nxt, N_MIX + k, u_hi[:, k, :])
                    if k % 4 == 3:
                        split_to(c, U_DOWN_B + 6 + k // 4)

            act.dma_start(vec[:, :], vectors).then_inc(vec_loaded, 16)
            act.dma_start(table[0:NUM_BUCKETS, :], rel_table).then_inc(vec_loaded, 16)
            act.dma_start(fix[:, :, :], fixed.rearrange("p (n k) -> p n k", n=2)).then_inc(vec_loaded, 16)
            act.dma_start(buckets, bucket_rows).then_inc(vec_loaded, 16)
            load_x(0)
            act.wait_ge(consts, 2)
            for u in range(3):
                split_one(u, 16 * (u // RAW_SLOTS + 1), None)
            for n in range(N_HEADS):
                act.wait_ge(row_done, n + 1)
                if n >= 2:
                    act.wait_ge(row_stored[n % 2], 16 * (n // 2))
                act.activation(row[:, n % 2, :], psum[:, n % 2, 0:REL], ACT.Copy).then_inc(row_copied, 1)
                act.wait_ge(row_copied, n + 1)
                act.dma_start(bias_rows[n, :, :], row[:, n % 2, :]).then_inc(row_stored[n % 2], 16)
            for s in range(2):
                act.wait_ge(row_stored[s], 16 * N_HEADS // 2)
            skewed = bias_rows.rearrange("n q m -> n (q m)")[:, P - 1:P - 1 + P * (REL - 1)] \
                              .rearrange("n (q m) -> q n m", m=REL - 1)[:, :, 0:2 * P]
            act.dma_start(bias[:, :, :], skewed).then_inc(bias_loaded, 16)
            act.wait_ge(x_loaded, 16)
            for k in range(KD):
                if k >= 2:
                    act.wait_ge(square_added, k - 1)
                act.activation(square[:, k % 2, :], x_in[:, k, :], ACT.Square).then_inc(square_ready, 1)
            deviation(0, ST_MIX, None)
            for k in range(KD):
                round_tile(0, N_MIX + k, u_hi[:, k, :])
            with act.Fori(0, CHUNKS - 1) as c:
                chunk(c, False)
            chunk(CHUNKS - 1, True)
            act.wait_ge(out_stored, CHUNKS * 2 * 16 + 1)

        @block.vector
        def _(dve):
            def add_squares(c, first, n):
                for t in range(n):
                    dve.wait_ge(square_ready, c * SQUARES + (first + t + 1))
                    add_square(first + t, t)

            def add_square(n, t):
                if t == 0:
                    dve.tensor_copy(square_sum[:, :], square[:, n % 2, :]).then_inc(square_added, 1)
                else:
                    dve.tensor_tensor(square_sum[:, :], square_sum[:, :], square[:, n % 2, :], ALU.add) \
                       .then_inc(square_added, 1)
                dve.drain()

            def reciprocal_of(c, index):
                dve.wait_ge(std_ready, c * STATS + (index + 1))
                dve.reciprocal(rstd[:, :], rstd[:, :])
                dve.drain()

            def scale_tile(c, n, tile, gain):
                return dve.scalar_tensor_tensor(normed[:, n % 2, :], tile, vec[:, gain:gain + 1], rstd[:, :],
                                                ALU.mult, ALU.mult).then_inc(normed_ready, 1)

            def rest_of(c, n, hi, lo):
                dve.wait_ge(hi_done, c * NORMED + (n + 1))
                dve.tensor_tensor(lo, normed[:, n % 2, :], hi.bitcast(F32), ALU.subtract).then_inc(lo_done, 1)

            def normalise(c, first, tiles, gain0, his, los):
                for t, tile in enumerate(tiles):
                    scale_tile(c, first + t, tile, gain0 + t)
                    if t >= 1:
                        rest_of(c, first + t - 1, his[t - 1], los[t - 1])
                        dve.drain()
                rest_of(c, first + len(tiles) - 1, his[-1], los[-1])
                dve.drain()

            def norm_mix(c):
                add_squares(c, Q_MIX, KD)
                reciprocal_of(c, ST_MIX)
                normalise(c, N_MIX, [x_in[:, k, :] for k in range(KD)], V_MIX_G,
                          [u_hi[:, k, :] for k in range(KD)], [u_lo[:, k, :] for k in range(KD)])

            def norm_qk(c, n, tile, gain, hi, lo):
                reciprocal_of(c, ST_K + n)
                scale_tile(c, N_K + n, psum[:, bank_of(tile), :], gain)
                dve.drain()
                dve.sem_inc(bank_free[bank_of(tile)], 1)
                rest_of(c, N_K + n, hi, lo)
                dve.drain()

            def softmax(c, m):
                hf = m % 2
                at = slice(4 * hf, 4 * hf + 4)
                dve.wait_ge(scores_done, c * HALVES + (m + 1))
                dve.scalar_tensor_tensor(scores.rearrange("p n k -> p (n k)"),
                                         psum[:, S_BANK:S_BANK + 2, :].rearrange("p n k -> p (n k)"),
                                         HEAD_DIM ** -0.5, bias[:, at, :].rearrange("p n k -> p (n k)"),
                                         ALU.mult, ALU.add)
                dve.drain()
                if m < 2:
                    dve.tensor_scalar(scores[:, :, 0:P], scores[:, :, 0:P], edge[:, :], None, ALU.add)
                    dve.drain()
                dve.tensor_reduce(top[:, at], scores, AXIS_X, ALU.max)
                dve.drain()
                sinks = vec[:, V_SINKS + 4 * hf:V_SINKS + 4 * hf + 4]
                dve.tensor_tensor(top[:, at], top[:, at], sinks, ALU.max)
                dve.drain()
                dve.tensor_scalar(neg_top[:, at], top[:, at], -1.0, None, ALU.mult)
                dve.tensor_tensor(sink_less[:, at], sinks, top[:, at], ALU.subtract).then_inc(top_ready, 1)
                if m == 1:
                    dve.memset(edge[:, :], 0.0)

            def divide_heads(c, i):
                dve.wait_ge(exp_done, c * HALVES + (2 * i + 2))
                total = denom[:, i % 2, :]
                dve.tensor_tensor(total, total, sink_exp[:, i % 2, :], ALU.add)
                dve.drain()
                dve.reciprocal(total, total)
                dve.drain()
                dve.wait_ge(pv_done, c * HALVES + (2 * i + 2))
                if i >= 1:
                    dve.wait_ge(heads_turned, c * BLOCKS + i)
                dve.tensor_tensor(heads.rearrange("p (n d) -> p n d", n=N_HEADS),
                                  psum[:, STAT_BANK, :].rearrange("p (n d) -> p n d", n=N_HEADS),
                                  total.rearrange("p (n o) -> p n o", o=1).broadcast_to([P, N_HEADS, HEAD_DIM]),
                                  ALU.mult).then_inc(heads_ready, 1)

            def conv_taps(c, j):
                dve.wait_ge(tap_done, c * CT + (j + 1))
                for k in (1, 0):
                    w = V_CONV_W + 3 * j + k
                    dve.scalar_tensor_tensor(conv, gated[:, j, k:k + T], vec[:, w:w + 1], conv, ALU.mult, ALU.add)
                    dve.drain()
                dve.tensor_copy(gated[:, j, 0:2], gated[:, j, T:T + 2])

            def up_phase(c, tile0, part, f0):
                with dve.Fori(0, part // 2) as i:
                    for e in range(2):
                        f = i * 2 + (f0 + e)
                        pair = c * FT + f
                        tail = up_tail[:, bass.ds(f, 1), :, :].rearrange("p a g t -> p (a g) t")
                        dve.wait_ge(up_copied, pair * 2 + 2)
                        for gv in range(2):
                            dve.sem_inc(bank_free[2 * e + gv], 1)
                        dve.tensor_copy(up[:, :, 0:2], tail)
                        dve.drain()
                        for k in (1, 0):
                            for gv in range(2):
                                w = vec[:, bass.ds(f * 8 + (V_FFN + gv * 4 + k), 1)]
                                dve.scalar_tensor_tensor(up_conv[:, gv, :], up[:, gv, k:k + T], w, up_conv[:, gv, :],
                                                         ALU.mult, ALU.add)
                            dve.drain()
                        dve.tensor_copy(tail, up[:, :, T:T + 2]).then_inc(conv_done, 1)
                        dve.wait_ge(silu_done, pair + 1)
                        dve.tensor_tensor(product32, up_conv[:, 0, :], up_conv[:, 1, :], ALU.mult) \
                           .then_inc(product_ready, 1)
                        dve.wait_ge(g_hi_done, pair + 1)
                        gh, gl = (g[:, bass.ds(i * 2 + e, 1), :].rearrange("p a t -> p (a t)") for g in (g_hi, g_lo))
                        dve.tensor_tensor(gl, product32, gh.bitcast(F32), ALU.subtract).then_inc(g_ready, 1)

            def add_to_h(c, tile0, ready=None):
                for d in range(KD):
                    dve.wait_ge(pe_done, c * EVENTS + (tile_end(tile0 + d) + 1))
                    add = dve.tensor_tensor(h[:, d, :], psum[:, bank_of(tile0 + d), :], h[:, d, :], ALU.add)
                    add.then_inc(bank_free[bank_of(tile0 + d)], 1)
                    dve.drain()
                    if ready is not None:
                        dve.sem_inc(ready, 1)

            def chunk(c, last):
                for k in (k_hi, k_lo):
                    dve.tensor_copy(k[:, 0:P], k[:, T:T + P].bitcast(F32))
                dve.tensor_copy(v_sb[:, 0, :], v_sb[:, BLOCKS, :])
                dve.drain()
                dve.sem_inc(tails_moved, 1)
                dve.wait_ge(v_copied, c + 1)
                dve.sem_inc(bank_free[bank_of(U_V)], 1)
                norm_qk(c, 0, U_K, V_K_G, k_hi[:, P:P + T], k_lo[:, P:P + T])
                for p in range(QT):
                    norm_qk(c, 1 + p, U_Q + p, V_Q_G, g_hi[:, KD + p, :], g_lo[:, KD + p, :])
                for m in range(-1, 3 * CT - 1):
                    n = m + 1
                    j, kind = n // 3, n % 3
                    tile = U_CONV + n
                    if kind == 0:
                        dve.wait_ge(c_copied, c * CT + (j + 1))
                        dve.sem_inc(bank_free[bank_of(tile)], 1)
                    elif kind == 1:
                        dve.wait_ge(pe_done, c * EVENTS + (tile_end(tile) + 1))
                        dve.tensor_tensor(gated[:, j, 2:2 + T], psum[:, bank_of(tile), :], gate_c, ALU.mult) \
                           .then_inc(gated_ready, 1)
                        dve.drain()
                        dve.sem_inc(bank_free[bank_of(tile)], 1)
                    else:
                        dve.wait_ge(pe_done, c * EVENTS + (tile_end(tile) + 1))
                        if j == 0:
                            dve.wait_ge(out_stored, c * 32 + 1)
                        dve.tensor_tensor(h[:, j, :], psum[:, bank_of(tile), :], conv, ALU.mult).then_inc(y_ready, 1)
                        dve.drain()
                        dve.sem_inc(bank_free[bank_of(tile)], 1)
                    if m < 0:
                        continue
                    if 2 <= m < HALVES + 2 and m % 2 == 1:
                        divide_heads(c, (m - 3) // 2)
                    if 1 <= m < HALVES + 1:
                        dve.wait_ge(turned, c * 2 * HALVES + (2 * m - 1))
                        dve.tensor_copy(probs_t[:, 0, :], psum[:, PT_BANKS[0], :]).then_inc(pt_first, 1)
                    if m < HALVES:
                        softmax(c, m)
                    if kind == 1:
                        conv_taps(c, j)
                    if kind == 2:
                        dve.wait_ge(square_ready, c * SQUARES + (Q_CONV + j + 1))
                        add_square(Q_CONV + j, j)
                branch = [h[:, k, :] for k in range(KD)]
                reciprocal_of(c, ST_CONV)
                add_squares(c, Q_ATTN, QT)
                normalise(c, N_CONV, branch[0:CT], V_CONV_G, [g_hi[:, k, :] for k in range(CT)],
                          [g_lo[:, k, :] for k in range(CT)])
                reciprocal_of(c, ST_ATTN)
                normalise(c, N_ATTN, branch[CT:KD], V_ATTN_G, [g_hi[:, k, :] for k in range(CT, KD)],
                          [g_lo[:, k, :] for k in range(CT, KD)])
                for d in range(KD):
                    tile = T_OUT + d
                    dve.wait_ge(pe_done, c * EVENTS + (tile_end(tile) + 1))
                    dve.tensor_tensor(h[:, d, :], psum[:, bank_of(tile), :], x_in[:, d, :], ALU.add) \
                       .then_inc(h_ready, 1)
                    dve.drain()
                    dve.sem_inc(bank_free[bank_of(tile)], 1)
                    if d >= 1:
                        dve.wait_ge(square_ready, c * SQUARES + (Q_FFN + d))
                        add_square(Q_FFN + d - 1, d - 1)
                dve.sem_inc(x_used, 1)
                dve.wait_ge(square_ready, c * SQUARES + (Q_FFN + KD))
                add_square(Q_FFN + KD - 1, KD - 1)
                reciprocal_of(c, ST_FFN)
                normalise(c, N_FFN, [h[:, k, :] for k in range(KD)], V_FFN_G,
                          [u_hi[:, k, :] for k in range(KD)], [u_lo[:, k, :] for k in range(KD)])
                up_phase(c, T_UP_A, PART_A, 0)
                add_to_h(c, T_DOWN_A)
                up_phase(c, T_UP_B, PART_B, PART_A)
                if not last:
                    norm_mix(c + 1)
                add_to_h(c, T_DOWN_B, out_ready)

            dve.memset(mean_model, 1.0 / D_MODEL)
            dve.memset(mean_branch, 1.0 / CONV_WIDTH)
            dve.memset(eps[:, :], EPS)
            dve.memset(edge[:, :], MASKED)
            dve.memset(k_hi[:, T:T + P].bitcast(F32), 0.0)
            dve.memset(k_lo[:, T:T + P].bitcast(F32), 0.0)
            dve.memset(v_sb[:, BLOCKS, :], 0.0)
            dve.memset(up_tail[:, :, :, :], 0.0)
            dve.memset(gated[:, :, 0:2], 0.0)
            dve.drain()
            dve.sem_inc(pe_done, 1)
            dve.sem_inc(out_stored, 1)
            for b in range(4):
                dve.sem_inc(bank_free[b], 1)
            dve.sem_inc(product_ready, 1)
            dve.sem_inc(consts, 2)
            dve.wait_ge(vec_loaded, 64)
            dve.memset(table[NUM_BUCKETS:NUM_BUCKETS + 1, :], 1.0)
            dve.drain()
            dve.tensor_copy(table_wide, table[:, :].rearrange("p (n o) -> p n o", o=1)
                            .broadcast_to([NUM_BUCKETS + 1, N_HEADS, P])).then_inc(wide_ready, 1)
            norm_mix(0)
            dve.wait_ge(bias_loaded, 16)
            with dve.Fori(0, CHUNKS - 1) as c:
                chunk(c, False)
            chunk(CHUNKS - 1, True)


def relative_buckets():
    a = np.zeros((NUM_BUCKETS + 1, REL), np.float32)
    for m in range(REL):
        d = 2 * P - 1 - m
        if 0 <= d < WINDOW:
            b = d
            if d >= MAX_EXACT:
                b = MAX_EXACT + int(math.log(d / MAX_EXACT) / math.log(MAX_DISTANCE / MAX_EXACT)
                                    * (NUM_BUCKETS - MAX_EXACT))
            a[min(b, NUM_BUCKETS - 1), m] = 1.0
        else:
            a[NUM_BUCKETS, m] = MASKED
    return a


def lay_out(a):
    a = {k: np.asarray(v) for k, v in a.items()}
    pairs = [n for p in range(QT) for n in (p, p + QT)]
    scored = [2 * f + n + QT * e for f in range(2) for e in range(2) for n in range(2)]
    x = a["x"][0].reshape(CHUNKS, T, KD, P).transpose(0, 3, 2, 1).reshape(CHUNKS, P, KD * T)

    def units(w, order):
        k, n = w.shape
        return w.reshape(k // P, P, n // P, P).transpose(2, 1, 0, 3)[order].reshape(len(order), P, k)

    w_in = a["w_in"][0]
    q0 = 3 * CONV_WIDTH
    q = w_in[:, q0:q0 + ATTN_WIDTH].reshape(D_MODEL, N_HEADS, HEAD_DIM)[:, pairs].reshape(D_MODEL, ATTN_WIDTH)
    w_in = np.concatenate([w_in[:, :q0], q, w_in[:, q0 + ATTN_WIDTH:]], axis=1)
    first = 3 * CT + QT
    order = [first, first + 1] + [3 * CT + p for p in range(QT)]
    for j in range(CT):
        order += [CT + j, 2 * CT + j, j]
    w_out = a["w_out"][0]
    w_attn = w_out[CONV_WIDTH:].reshape(N_HEADS, HEAD_DIM, D_MODEL)[scored].reshape(ATTN_WIDTH, D_MODEL)
    w_out = np.concatenate([w_out[:CONV_WIDTH], w_attn])
    w_up, w_down = a["w_up"][0], a["w_down"][0]

    def up(f0, n):
        return units(w_up, [g * FT + f for f in range(f0, f0 + n) for g in range(2)])

    def down(f0, n):
        w = w_down.reshape(FT, P, KD, P)[f0:f0 + n].transpose(2, 0, 1, 3).reshape(n * KD // 8, 8, P, P)
        return w.transpose(0, 2, 1, 3).reshape(n * KD // 8, P, 8 * P)

    weights = np.concatenate([units(w_in, order), units(w_out, list(range(KD))),
                              up(0, PART_A), down(0, PART_A), up(PART_A, PART_B), down(PART_A, PART_B)])

    def columns(v):
        return v.reshape(-1, P).T

    conv = a["conv_w"][0].reshape(3, CT, P).transpose(2, 1, 0).reshape(P, 3 * CT)
    taps = np.concatenate([a["ffn_conv_w"][0], a["ffn_conv_b"]]).reshape(4, 2, FT, P)
    attn_g = a["out_norm_attn_g"][0].reshape(N_HEADS, HEAD_DIM)[scored].reshape(-1)
    vectors = np.concatenate([
        columns(a["norm_mix_g"][0]), columns(a["norm_ffn_g"][0]), columns(a["out_norm_conv_g"][0]), columns(attn_g),
        columns(np.tile(a["q_norm_g"][0], 2)), columns(np.tile(a["k_norm_g"][0], 2)), conv,
        np.broadcast_to(a["sinks"][0][scored], (P, N_HEADS)),
        taps.transpose(3, 2, 1, 0).reshape(P, FT * 8)], axis=1)
    same_head = np.kron(np.eye(2), np.ones((HEAD_DIM, HEAD_DIM))) / HEAD_DIM
    fixed = np.concatenate([np.eye(P), same_head], axis=1).astype(np.float32)
    out = {"x": x, "weights": weights, "vectors": vectors, "rel_table": a["rel_bias_table"][:, scored],
           "fixed": fixed, "bucket_rows": relative_buckets()}
    return {k: np.ascontiguousarray(v) for k, v in out.items()}


def kernel(**inputs):
    import concourse.bacc as bacc
    from concourse.bass_utils import run_bass_kernel_spmd

    nc = bacc.Bacc("TRN2", target_bir_lowering=False, num_devices=1)
    arrays = lay_out(inputs)
    args = [nc.dram_tensor(n, a.shape, F32, kind="ExternalInput").ap() for n, a in arrays.items()]
    bias_rows = nc.dram_tensor("bias_rows", (N_HEADS, P, REL), F32, kind="Internal").ap()
    out = nc.dram_tensor("out", (CHUNKS, P, KD * T), F32, kind="ExternalOutput").ap()
    build_layer(nc, *args, bias_rows, out)
    result = run_bass_kernel_spmd(nc, [arrays], core_ids=[0]).results[0]["out"]
    return result.reshape(CHUNKS, P, KD, T).transpose(0, 3, 2, 1).reshape(1, SEQ, D_MODEL)
```

```python
import math
from contextlib import ExitStack

import numpy as np

import concourse.bass as bass
from concourse import mybir

F32 = mybir.dt.float32
F32R = mybir.dt.float32r
ACT = mybir.ActivationFunctionType
ALU = mybir.AluOpType
LN_EXP_SET, SILU_SET = "natural_log_exp_and_others", "silu_and_others"
AXIS_X = mybir.AxisListType.X

P = 128
D_MODEL, SEQ = 1024, 2048
CONV_WIDTH, ATTN_WIDTH, HEAD_DIM, N_HEADS, N_KV = 512, 512, 64, 8, 2
KV_WIDTH = N_KV * HEAD_DIM
D_FF = 2816
NUM_BUCKETS, MAX_DISTANCE, WINDOW = 32, 128, 128
MAX_EXACT = NUM_BUCKETS // 2
EPS = 1e-6
MASKED = -1e30

T = 512
CHUNKS = SEQ // T
KD = D_MODEL // P
QT = N_HEADS // 2
CT = CONV_WIDTH // P
BLOCKS = T // P
HALVES = 2 * BLOCKS
FT = D_FF // P
PART_A, PART_B = 12, 10
SLOTS = 4
RAW_SLOTS = 2

U_K, U_V, U_Q, U_CONV = 0, 1, 2, 2 + QT
U_OUT = U_CONV + 3 * CT
U_UP_A = U_OUT + KD
U_DOWN_A = U_UP_A + 2 * PART_A
U_UP_B = U_DOWN_A + PART_A * KD // 8
U_DOWN_B = U_UP_B + 2 * PART_B
UNITS = U_DOWN_B + PART_B * KD // 8

T_OUT = U_OUT
T_UP_A = T_OUT + KD
T_DOWN_A = T_UP_A + 2 * PART_A
T_UP_B = T_DOWN_A + KD
T_DOWN_B = T_UP_B + 2 * PART_B
TILES = T_DOWN_B + KD

DOWN_ENDS = {n: sorted({k for k in range(1, n * KD + 1) if k % 8 == 0 or k % n == 0}) for n in (PART_A, PART_B)}
E_DOWN_A = U_DOWN_A
E_UP_B = E_DOWN_A + len(DOWN_ENDS[PART_A])
E_DOWN_B = E_UP_B + 2 * PART_B
EVENTS = E_DOWN_B + len(DOWN_ENDS[PART_B])


def unit_end(u):
    for unit0, event0, part in ((U_DOWN_B, E_DOWN_B, PART_B), (U_DOWN_A, E_DOWN_A, PART_A)):
        if unit0 <= u < unit0 + part * KD // 8:
            return event0 + DOWN_ENDS[part].index(8 * (u - unit0 + 1)) + 1
    return (u + 1) if u < U_DOWN_A else E_UP_B + (u - U_UP_B) + 1


def tile_end(t):
    for tile0, event0, part in ((T_DOWN_B, E_DOWN_B, PART_B), (T_DOWN_A, E_DOWN_A, PART_A)):
        if tile0 <= t < tile0 + KD:
            return event0 + DOWN_ENDS[part].index(part * (t - tile0 + 1)) + 1
    return (t + 1) if t < T_DOWN_A else E_UP_B + (t - T_UP_B) + 1


ST_MIX, ST_K, ST_Q, ST_ATTN, ST_CONV, ST_FFN = 0, 1, 2, 2 + QT, 3 + QT, 4 + QT
STATS = 5 + QT
N_MIX, N_K, N_Q = 0, KD, KD + 1
NORMED = N_Q + QT
Q_MIX, Q_CONV = 0, KD
Q_FFN = Q_CONV + CT
SQUARES = Q_FFN + KD
BANK_USES = ([(t, 0, t) for t in range(U_CONV)] + [(t, 0, t % 3) for t in range(U_CONV, T_OUT)]
             + [(T_OUT + d, part, 3 * part + d % 3) for d in range(KD) for part in range(2)]
             + [(t, 0, (t - first) % 4) for first, end in
                ((T_UP_A, T_DOWN_A), (T_DOWN_A, T_UP_B), (T_UP_B, T_DOWN_B), (T_DOWN_B, TILES))
                for t in range(first, end)])
BANKS = 6
USES = [sum(bank == b for _, _, bank in BANK_USES) for b in range(BANKS)]


def bank_of(tile, part=0):
    return next(b for t, p, b in BANK_USES if (t, p) == (tile, part))


def uses_before(tile, part=0):
    at = next(n for n, (t, p, _) in enumerate(BANK_USES) if (t, p) == (tile, part))
    return sum(b == bank_of(tile, part) for _, _, b in BANK_USES[:at])


V_MIX_G, V_FFN_G = 0, KD
V_CONV_G = 2 * KD
V_ATTN_G = V_CONV_G + CT
V_Q_G = V_ATTN_G + QT
V_K_G = V_Q_G + 1
V_CONV_W = V_K_G + 1
V_SINKS = V_CONV_W + 3 * CT
V_FFN = V_SINKS + N_HEADS
V_COLS = V_FFN + FT * 2 * 4
REL = 3 * P


def build_layer(nc, x, weights, vectors, rel_table, fixed, bucket_rows, bias_rows, out):
    ctx = ExitStack()
    with ctx:
        def sb(name, shape, dt=F32):
            return ctx.enter_context(nc.sbuf_tensor(name, shape, dt))

        def sem(name):
            return ctx.enter_context(nc.semaphore(name))

        w_raw = sb("w_raw", [P, RAW_SLOTS, KD * P])
        w_hi = sb("w_hi", [P, SLOTS, KD * P], F32R)
        w_lo = sb("w_lo", [P, SLOTS, KD * P], F32R)
        x_in = sb("x_in", [P, KD, T])
        h = sb("h", [P, KD, T])
        u_hi = sb("u_hi", [P, KD, T], F32R)
        u_lo = sb("u_lo", [P, KD, T], F32R)
        g_hi = sb("g_hi", [P, PART_A, T], F32R)
        g_lo = sb("g_lo", [P, PART_A, T], F32R)
        k_hi = sb("k_hi", [P, P + T], F32R)
        k_lo = sb("k_lo", [P, P + T], F32R)
        v_sb = sb("v_sb", [P, 1 + BLOCKS, P])
        gated = sb("gated", [P, CT, 2 + T])
        up_tail = sb("up_tail", [P, FT, 2, 2])
        square = sb("square", [P, 2, T])
        square_sum = sb("square_sum", [P, T])
        rstd = sb("rstd", [P, T])
        rstd_attn = sb("rstd_attn", [P, T])
        normed = sb("normed", [P, 2, T])
        shared = sb("shared", [P, 7 * T])
        scores = shared[:, 0:2 * T].rearrange("p (n k) -> p n k", n=4)
        probs_t = shared[:, 2 * T:4 * T].rearrange("p (n k) -> p n k", n=2)
        gate_c = shared[:, 4 * T:5 * T]
        conv = shared[:, 5 * T:6 * T]
        heads = shared[:, 6 * T:7 * T]
        v_t = conv
        up_conv = shared[:, 0:2 * T].rearrange("p (n t) -> p n t", n=2)
        product32 = shared[:, 2 * T:3 * T]
        up = shared[:, 3 * T:5 * T + 4].rearrange("p (n t) -> p n t", n=2)
        bias = sb("bias", [P, N_HEADS, 2 * P])
        vec = sb("vec", [P, V_COLS])
        table = sb("table", [NUM_BUCKETS + 1, N_HEADS])
        fix = sb("fix", [P, 2, P])
        mean_model = sb("mean_model", [P, P])[:, :]
        mean_branch = sb("mean_branch", [P, P])[:, :]
        edge = sb("edge", [P, 1])
        eps = sb("eps", [P, 1])
        top = sb("top", [P, N_HEADS])
        neg_sinks = sb("neg_sinks", [P, N_HEADS])
        head_squares = sb("head_squares", [P, BLOCKS])
        neg_top = sb("neg_top", [P, N_HEADS])
        sink_less = sb("sink_less", [P, N_HEADS])
        sink_exp = sb("sink_exp", [P, 2, N_HEADS])
        denom = sb("denom", [P, 2, N_HEADS])
        identity, mean_head = fix[:, 0, :], fix[:, 1, :]
        table_wide = shared[0:NUM_BUCKETS + 1, 0:N_HEADS * P].rearrange("p (n k) -> p n k", n=N_HEADS)
        buckets = shared[0:NUM_BUCKETS + 1, 2 * T:2 * T + REL]
        rows = h[:, 0:REL * N_HEADS // T, :].rearrange("p k t -> p (k t)").rearrange("p (n m) -> p n m", n=N_HEADS)

        psum = ctx.enter_context(nc.psum_tensor("psum", [P, 8, T], F32))
        S_BANK, PT_BANKS, STAT_BANK = 4, (6, 3), 7

        w_loaded = [sem(f"w_loaded{s}") for s in range(RAW_SLOTS)]
        w_hi_done, w_ready = sem("w_hi_done"), sem("w_ready")
        pe_done = sem("pe_done")
        bank_free = [sem(f"bank_free{b}") for b in range(BANKS)]
        stat_done, stat_read, rstd_ready = sem("stat_done"), sem("stat_read"), sem("rstd_ready")
        qk_square = sem("qk_square")
        square_ready, square_added = sem("square_ready"), sem("square_added")
        normed_ready, hi_done, lo_done = sem("normed_ready"), sem("hi_done"), sem("lo_done")
        v_copied, v_turned, v_ready, tails_moved = sem("v_copied"), sem("v_turned"), sem("v_ready"), sem("tails_moved")
        scores_done, top_ready, exp_done = sem("scores_done"), sem("top_ready"), sem("exp_done")
        turned, pt_first, pt_second = sem("turned"), sem("pt_first"), sem("pt_second")
        pv_done, heads_ready = sem("pv_done"), sem("heads_ready")
        heads_squared = sem("heads_squared")
        heads_turned, heads_hi_done, attn_split = sem("heads_turned"), sem("heads_hi_done"), sem("attn_split")
        c_copied, gated_ready, tap_done, y_ready = sem("c_copied"), sem("gated_ready"), sem("tap_done"), sem("y_ready")
        y_hi_done, conv_split = sem("y_hi_done"), sem("conv_split")
        h_ready, h_hi_done, h_split = sem("h_ready"), sem("h_hi_done"), sem("h_split")
        gate_ready, silu_done = sem("gate_ready"), sem("silu_done")
        product_ready, g_hi_done, g_ready = sem("product_ready"), sem("g_hi_done"), sem("g_ready")
        first_loaded = [sem(f"first_loaded{n}") for n in range(2)]
        x_loaded, out_ready, out_stored = sem("x_loaded"), sem("out_ready"), sem("out_stored")
        consts, vec_loaded = sem("consts"), sem("vec_loaded")
        wide_ready, rows_done, rows_copied = sem("wide_ready"), sem("rows_done"), sem("rows_copied")
        rows_stored, bias_loaded = sem("rows_stored"), sem("bias_loaded")
        sink_ready = sem("sink_ready")

        block = ctx.enter_context(nc.Block())

        @block.sync
        def _(sp):
            def load(unit, slot):
                sp.dma_start(w_raw[:, slot, :], weights[bass.ds(unit, 1), :, :].rearrange("a p n -> p (a n)")) \
                  .then_inc(w_loaded[slot], 16)

            sp.dma_start(table[0:NUM_BUCKETS, :], rel_table).then_inc(vec_loaded, 16)
            sp.dma_start(buckets, bucket_rows).then_inc(vec_loaded, 16)
            sp.dma_start(vec[:, :], vectors).then_inc(vec_loaded, 16)
            sp.dma_start(fix[:, :, :], fixed.rearrange("p (n k) -> p n k", n=2)).then_inc(vec_loaded, 16)
            for n in range(2):
                half = slice(n * KD // 2, (n + 1) * KD // 2)
                sp.dma_start(x_in[:, half, :],
                             x[0:1, :, half.start * T:half.stop * T].rearrange("a p (k t) -> p (a k) t", t=T)) \
                  .then_inc(first_loaded[n], 16)
            for s in range(RAW_SLOTS):
                load(s, s)
            sp.wait_ge(rows_copied, 2)
            sp.dma_start(bias_rows.rearrange("n q m -> q n m"), rows).then_inc(rows_stored, 16)
            for s in range(RAW_SLOTS):
                sp.wait_ge(w_ready, s + 1)
                load(RAW_SLOTS + s, s)
            sp.wait_ge(rows_stored, 16)
            skewed = bias_rows.rearrange("n q m -> n (q m)")[:, P - 1:P - 1 + P * (REL - 1)] \
                              .rearrange("n (q m) -> q n m", m=REL - 1)[:, :, 0:2 * P]
            sp.dma_start(bias[:, :, :], skewed).then_inc(bias_loaded, 16)
            with sp.Fori(2, UNITS // RAW_SLOTS) as i:
                for s in range(RAW_SLOTS):
                    unit = sp.snap(i * RAW_SLOTS + s)
                    sp.wait_ge(w_ready, i * RAW_SLOTS + (s + 1 - RAW_SLOTS))
                    load(unit, s)
            with sp.Fori(1, CHUNKS) as c:
                with sp.Fori(0, UNITS // RAW_SLOTS) as i:
                    for s in range(RAW_SLOTS):
                        unit = sp.snap(i * RAW_SLOTS + s)
                        sp.wait_ge(w_ready, c * UNITS + i * RAW_SLOTS + (s + 1 - RAW_SLOTS))
                        load(unit, s)

        @block.gpsimd
        def _(pool):
            with pool.Fori(0, CHUNKS * UNITS // SLOTS) as i:
                for s in range(SLOTS):
                    pool.wait_ge(w_hi_done, i * SLOTS + (s + 1))
                    pool.tensor_tensor(w_lo[:, s, :], w_raw[:, s % RAW_SLOTS, :], w_hi[:, s, :].bitcast(F32),
                                       ALU.subtract).then_inc(w_ready, 1)

        @block.tensor
        def _(pe):
            def product(bank, free, pairs, middle=None, event=True):
                pe.wait_ge(bank_free[bank], free)
                seen = None
                for n, (unit, name, k, last_use, a_hi, a_lo, waits) in enumerate(pairs):
                    if name != seen:
                        pe.wait_ge(w_ready, unit + 1)
                        seen = name
                    for s, v in waits:
                        pe.wait_ge(s, v)
                    slot = name % SLOTS
                    hi, lo = w_hi[:, slot, k * P:(k + 1) * P], w_lo[:, slot, k * P:(k + 1) * P]
                    end = n == len(pairs) - 1
                    pe.matmul(psum[:, bank, :], hi, a_hi, start=n == 0, stop=False)
                    pe.matmul(psum[:, bank, :], hi, a_lo, start=False, stop=False)
                    mm = pe.matmul(psum[:, bank, :], lo, a_hi, start=False, stop=end)
                    if last_use or (end and event):
                        mm.then_inc(pe_done, 1)
                    if middle and n == len(pairs) // 2 - 1:
                        middle()

            def projection(c, tile, unit, name, a_hi, a_lo, first=None, middle=None, free=None, bank=None):
                pairs = [(unit, name, k, k == KD - 1, a_hi[:, k, :], a_lo[:, k, :],
                          [(first[0], first[1] + k + 1)] if first is not None else []) for k in range(KD)]
                bank = bank_of(tile) if bank is None else bank
                free = c * USES[bank] + (uses_before(tile) + 1) if free is None else free
                product(bank, free, pairs, middle)

            def branch_part(c, d, part, ends):
                tile, u = T_OUT + d, U_OUT + d
                split, each = ((conv_split, CT), (attn_split, BLOCKS))[part]
                ks = range(part * CT, (part + 1) * CT)
                pairs = [(c * UNITS + u, u, k, False, g_hi[:, k, :], g_lo[:, k, :],
                          [] if d else [(split, c * each + (k % CT + 1 if part == 0 else each))]) for k in ks]
                bank = bank_of(tile, part)
                product(bank, c * USES[bank] + (uses_before(tile, part) + 1), pairs, event=ends)

            def head_statistic(c):
                pe.wait_ge(heads_squared, c * BLOCKS + BLOCKS)
                pe.wait_ge(stat_read, c * STATS + ST_ATTN)
                for i in range(BLOCKS):
                    mm = pe.matmul(psum[:, STAT_BANK, i * P:(i + 1) * P],
                                   head_squares[:, i:i + 1].broadcast_to([P, P]), identity, start=True, stop=True)
                mm.then_inc(stat_done, 1)

            def statistic(c, index, ready, value, mean, squares):
                pe.wait_ge(ready, value)
                if not (isinstance(c, int) and c == 0 and index == 0):
                    pe.wait_ge(stat_read, c * STATS + index)
                pe.matmul(psum[:, STAT_BANK, :], mean, squares, start=True, stop=True).then_inc(stat_done, 1)

            def qk_statistic(c, n):
                statistic(c, ST_K + n, qk_square, c * (1 + QT) + (n + 1), mean_head, square[:, 0, :])

            def turn_v(c):
                pe.wait_ge(v_copied, c + 1)
                for b in range(BLOCKS):
                    mm = pe.transpose(psum[:, PT_BANKS[0], b * P:(b + 1) * P], v_t[:, b * P:(b + 1) * P], identity)
                mm.then_inc(v_turned, 1)

            def score(c, m):
                i, hf = m // 2, m % 2
                if m == 0:
                    pe.wait_ge(lo_done, c * NORMED + NORMED)
                    for b in (S_BANK, S_BANK + 1):
                        pe.wait_ge(bank_free[b], c * USES[b] + (uses_before(T_OUT + b - 3, 1) + 1))
                for n in range(2):
                    p = 2 * hf + n
                    for e in range(2):
                        rows = slice(e * HEAD_DIM, (e + 1) * HEAD_DIM)
                        o = psum[:, S_BANK + e, n * 2 * P:(n + 1) * 2 * P]
                        qh, ql = (g[rows, KD + p, i * P:(i + 1) * P] for g in (g_hi, g_lo))
                        kh, kl = (k[rows, i * P:(i + 2) * P] for k in (k_hi, k_lo))
                        pe.matmul(o, qh, kh, start=True, stop=False)
                        pe.matmul(o, qh, kl, start=False, stop=False)
                        mm = pe.matmul(o, ql, kh, start=False, stop=True)
                mm.then_inc(scores_done, 1)

            def turn_probs(c, m):
                pe.wait_ge(exp_done, c * HALVES + (m + 1))
                if m == 0:
                    pe.wait_ge(v_ready, c + 1)
                    pe.wait_ge(bank_free[3], c * USES[3] + (uses_before(T_OUT, 1) + 1))
                if m % 2 == 1 and m >= 3:
                    pe.wait_ge(attn_split, c * BLOCKS + (m - 1) // 2)
                for e in range(2):
                    for n in range(2):
                        for kt in range(2):
                            at = 2 * n + kt
                            mm = pe.transpose(psum[:, PT_BANKS[e], at * P:(at + 1) * P],
                                              scores[:, 2 * e + n, kt * P:(kt + 1) * P], identity)
                    mm.then_inc(turned, 1)

            def weigh_values(c, m):
                i, hf = m // 2, m % 2
                pe.wait_ge(pt_first, c * HALVES + (m + 1))
                pe.wait_ge(pt_second, c * HALVES + (m + 1))
                if m == 0:
                    pe.wait_ge(stat_read, c * STATS + ST_ATTN)
                elif hf == 0:
                    pe.wait_ge(heads_ready, c * BLOCKS + i)
                for e in range(2):
                    for n in range(2):
                        at = (4 * hf + 2 * e + n) * HEAD_DIM
                        for kt in range(2):
                            mm = pe.matmul(psum[:, STAT_BANK, at:at + HEAD_DIM],
                                           probs_t[:, e, (2 * n + kt) * P:(2 * n + kt + 1) * P],
                                           v_sb[:, i + kt, e * HEAD_DIM:(e + 1) * HEAD_DIM],
                                           start=kt == 0, stop=kt == 1)
                mm.then_inc(pv_done, 1)

            def turn_heads(c, i):
                pe.wait_ge(heads_ready, c * BLOCKS + (i + 1))
                pe.wait_ge(pt_first, c * HALVES + min(2 * i + 3, HALVES))
                for p in range(QT):
                    mm = pe.transpose(psum[:, PT_BANKS[0], p * P:(p + 1) * P], heads[:, p * P:(p + 1) * P], identity)
                mm.then_inc(heads_turned, 1)

            def attention_step(c, m):
                if 2 <= m < HALVES + 2:
                    weigh_values(c, m - 2)
                if 1 <= m < HALVES + 1:
                    turn_probs(c, m - 1)
                if m < HALVES:
                    score(c, m)

            def up_projection(c, tile0, unit0, part, first=None, start=0):
                with pe.Fori(start, part // 2) as i:
                    for n in range(4):
                        projection(c, tile0 + n, c * UNITS + i * 4 + (unit0 + n), unit0 + n, u_hi, u_lo,
                                   free=c * USES[n] + i + (uses_before(tile0 + n) + 1), bank=n)

            def down_projection(c, tile0, unit0, part, g0, middle=None):
                for d in range(KD):
                    pairs = []
                    for k in range(part):
                        at = d * part + k
                        pairs.append((c * UNITS + (unit0 + at // 8), unit0 + at // 8, at % 8,
                                      at % 8 == 7, g_hi[:, k, :], g_lo[:, k, :],
                                      [(g_ready, c * FT + (g0 + k + 1))] if d == 0 else []))
                    bank = bank_of(tile0 + d)
                    product(bank, c * USES[bank] + (uses_before(tile0 + d) + 1), pairs,
                            middle if d == 2 else None)

            def chunk(c, last):
                def unit(n):
                    return c * UNITS + n

                projection(c, U_K, unit(U_K), U_K, u_hi, u_lo, first=(lo_done, c * NORMED + N_MIX))
                projection(c, U_V, unit(U_V), U_V, u_hi, u_lo, middle=lambda: qk_statistic(c, 0))
                projection(c, U_Q, unit(U_Q), U_Q, u_hi, u_lo, middle=lambda: turn_v(c))
                for p in range(1, QT):
                    projection(c, U_Q + p, unit(U_Q + p), U_Q + p, u_hi, u_lo,
                               middle=lambda p=p: qk_statistic(c, p))
                projection(c, U_CONV, unit(U_CONV), U_CONV, u_hi, u_lo, middle=lambda: qk_statistic(c, QT))
                for m in range(3 * CT - 1):
                    projection(c, U_CONV + 1 + m, unit(U_CONV + 1 + m), U_CONV + 1 + m, u_hi, u_lo,
                               middle=(lambda: turn_heads(c, m // 2 - 2)) if m >= 4 and m % 2 == 0 else None)
                    attention_step(c, m)
                branch_part(c, 0, 1, False)
                head_statistic(c)
                branch_part(c, 1, 1, False)
                branch_part(c, 2, 1, False)
                statistic(c, ST_CONV, square_added, c * SQUARES + Q_FFN, mean_branch, square_sum[:, :])
                for d in range(KD):
                    if d >= 3:
                        branch_part(c, d, 1, False)
                    branch_part(c, d, 0, True)
                for n in range(4):
                    projection(c, T_UP_A + n, unit(U_UP_A + n), U_UP_A + n, u_hi, u_lo,
                               first=(h_split, c * KD) if n == 0 else None,
                               middle=None if n != 1 else lambda: statistic(
                                   c, ST_FFN, square_added, c * SQUARES + SQUARES, mean_model, square_sum[:, :]))
                up_projection(c, T_UP_A, U_UP_A, PART_A, start=1)
                down_projection(c, T_DOWN_A, U_DOWN_A, PART_A, 0)
                up_projection(c, T_UP_B, U_UP_B, PART_B)
                nxt = c + 1
                down_projection(c, T_DOWN_B, U_DOWN_B, PART_B, PART_A,
                                None if last else lambda: statistic(nxt, ST_MIX, square_added,
                                                                    nxt * SQUARES + Q_CONV, mean_model,
                                                                    square_sum[:, :]))

            pe.wait_ge(consts, 2)
            pe.wait_ge(vec_loaded, 64)
            pe.wait_ge(wide_ready, 1)
            for n in range(N_HEADS):
                mm = pe.matmul(psum[:, n, 0:REL], table_wide[:, n, :], buckets, start=True, stop=True)
            mm.then_inc(rows_done, 1)
            pe.wait_ge(rows_copied, 2)
            statistic(0, ST_MIX, square_added, Q_CONV, mean_model, square_sum[:, :])
            with pe.Fori(0, CHUNKS - 1) as c:
                chunk(c, False)
            chunk(CHUNKS - 1, True)

        @block.scalar
        def _(act):
            state = [0]

            def split_to(c, n):
                while state[0] < n:
                    u = state[0]
                    before = unit_end(u - SLOTS) if u >= SLOTS else unit_end(u - SLOTS + UNITS) - EVENTS
                    split_one(u, c * (UNITS // RAW_SLOTS) * 16 + 16 * (u // RAW_SLOTS + 1),
                              c * EVENTS + (before + 1))
                    state[0] += 1

            def split_one(name, loads, used):
                slot, raw = name % SLOTS, name % RAW_SLOTS
                act.wait_ge(w_loaded[raw], loads)
                if used is not None:
                    act.wait_ge(pe_done, used)
                act.activation(w_hi[:, slot, :], w_raw[:, raw, :], ACT.Copy).then_inc(w_hi_done, 1)

            def root_of(c, index, used, into=rstd, scale=1.0):
                act.wait_ge(stat_done, c * STATS + (index + 1))
                if used is not None:
                    act.wait_ge(*used)
                act.activation(into[:, :], psum[:, STAT_BANK, :], ACT.Ln, bias=eps[:, :], scale=scale) \
                   .then_inc(stat_read, 1)
                act.drain()
                act.activation(into[:, :], into[:, :], ACT.Exp, scale=-0.5).then_inc(rstd_ready, 1)

            def round_tile(c, n, target):
                act.wait_ge(normed_ready, c * NORMED + (n + 1))
                act.activation(target, normed[:, n % 2, :], ACT.Copy).then_inc(hi_done, 1)

            def done(c, tile):
                act.wait_ge(pe_done, c * EVENTS + (tile_end(tile) + 1))

            def load_x(c):
                act.dma_start(x_in[:, :, :], x[bass.ds(c, 1), :, :].rearrange("a p (k t) -> p (a k) t", k=KD)) \
                   .then_inc(x_loaded, 16)

            def qk_square_of(c, n, tile):
                done(c, tile)
                act.activation(square[:, 0, :], psum[:, bank_of(tile), :], ACT.Square).then_inc(qk_square, 1)

            def exps(c, m):
                hf = m % 2
                act.wait_ge(top_ready, c * HALVES + (m + 1))
                for n in range(4):
                    at = 4 * hf + n
                    act.activation(scores[:, n, :], scores[:, n, :], ACT.Exp, bias=neg_top[:, at:at + 1],
                                   accum_out=denom[:, m // 2 % 2, at:at + 1])
                act.wait_ge(sink_ready, c * HALVES + (m + 1))
                act.activation(sink_exp[:, m // 2 % 2, 4 * hf:4 * hf + 4], sink_less[:, 4 * hf:4 * hf + 4], ACT.Exp) \
                   .then_inc(exp_done, 1)

            def attention_step(c, m):
                if 1 <= m < HALVES + 1:
                    act.wait_ge(turned, c * 2 * HALVES + 2 * m)
                    act.activation(probs_t[:, 1, :], psum[:, PT_BANKS[1], :], ACT.Copy).then_inc(pt_second, 1)
                if m >= 3 and m % 2 == 1 and m < HALVES + 2:
                    i = m // 2 - 1
                    act.wait_ge(heads_turned, c * BLOCKS + (i + 1))
                    for p in range(QT):
                        gain = vec[:, V_ATTN_G + p:V_ATTN_G + p + 1]
                        hi = act.activation(g_hi[:, CT + p, i * P:(i + 1) * P],
                                            psum[:, PT_BANKS[0], p * P:(p + 1) * P], ACT.Copy, scale=gain)
                    hi.then_inc(heads_hi_done, 1)
                if m < HALVES:
                    exps(c, m)
                if m >= 3 and m % 2 == 1 and m < HALVES + 2:
                    act.wait_ge(heads_ready, c * BLOCKS + (i + 1))
                    act.activation(rstd_attn[:, :], heads, ACT.Square, accum_out=head_squares[:, i:i + 1])
                    act.drain()
                    act.sem_inc(heads_squared, 1)

            def conv_step(c, n):
                j, kind = n // 3, n % 3
                if kind == 0:
                    done(c, U_CONV + n)
                    if j >= 1:
                        act.wait_ge(gated_ready, c * CT + j)
                    act.activation(gate_c, psum[:, bank_of(U_CONV + n), :], ACT.Copy).then_inc(c_copied, 1)
                if kind == 1:
                    act.wait_ge(gated_ready, c * CT + (j + 1))
                    if j >= 1:
                        act.wait_ge(y_ready, c * CT + j)
                    w = V_CONV_W + 3 * j + 2
                    act.activation(conv, gated[:, j, 2:2 + T], ACT.Copy, scale=vec[:, w:w + 1]).then_inc(tap_done, 1)

            def up_phase(c, tile0, unit0, part, f0):
                with act.Fori(0, part // 2) as i:
                    for e in range(2):
                        pair = c * FT + i * 2 + (f0 + e)
                        for gv in range(2):
                            n = 2 * e + gv
                            split_one(unit0 + n + 3, c * (UNITS // RAW_SLOTS * 16) + i * (4 // RAW_SLOTS * 16)
                                      + ((unit0 + n + 3) // RAW_SLOTS + 1) * 16,
                                      c * EVENTS + i * 4 + (tile_end(tile0 + n)))
                        act.wait_ge(gate_ready, pair + 1)
                        act.activation(up_conv[:, 0, :], up_conv[:, 0, :], ACT.Silu).then_inc(silu_done, 1)
                        act.wait_ge(product_ready, pair + 1)
                        act.activation(g_hi[:, bass.ds(i * 2 + e, 1), :].rearrange("p a t -> p (a t)"),
                                       product32, ACT.Copy).then_inc(g_hi_done, 1)
                state[0] += 2 * part

            def chunk(c, last):
                state[0] = 3
                split_to(c, 4)
                qk_square_of(c, 0, U_K)
                split_to(c, 5)
                done(c, U_V)
                act.wait_ge(tails_moved, c + 1)
                act.activation(v_t, psum[:, bank_of(U_V), :], ACT.Copy).then_inc(v_copied, 1)
                root_of(c, ST_K, (normed_ready, c * NORMED + N_K))
                round_tile(c, N_K, k_hi[:, P:P + T])
                split_to(c, 6)
                qk_square_of(c, 1, U_Q)
                act.wait_ge(v_turned, c + 1)
                act.activation(v_sb[:, 1:1 + BLOCKS, :],
                               psum[:, PT_BANKS[0], :].rearrange("p (b d) -> p b d", b=BLOCKS), ACT.Copy) \
                   .then_inc(v_ready, 1)
                for p in range(QT):
                    split_to(c, 7 + p)
                    root_of(c, ST_Q + p, (normed_ready, c * NORMED + N_Q + p))
                    round_tile(c, N_Q + p, g_hi[:, KD + p, :])
                    if p + 1 < QT:
                        qk_square_of(c, 2 + p, U_Q + p + 1)
                conv_step(c, 0)
                for m in range(3 * CT - 1):
                    conv_step(c, 1 + m)
                    attention_step(c, m)
                    split_to(c, U_CONV + 1 + m + 4)
                    if (1 + m) % 3 == 2:
                        j = (1 + m) // 3
                        act.wait_ge(y_ready, c * CT + (j + 1))
                        gain = vec[:, V_CONV_G + j:V_CONV_G + j + 1]
                        act.activation(g_hi[:, j, :], normed[:, j % 2, :], ACT.Copy, scale=gain).then_inc(y_hi_done, 1)
                        square_tile(c, Q_CONV + j, normed[:, j % 2, :])
                root_of(c, ST_ATTN, None, rstd_attn, 1.0 / ATTN_WIDTH)
                root_of(c, ST_CONV, (normed_ready, c * NORMED + NORMED))
                for d in range(KD):
                    split_to(c, U_OUT + d + 4)
                    act.wait_ge(h_ready, c * KD + (d + 1))
                    gain = vec[:, V_FFN_G + d:V_FFN_G + d + 1]
                    act.activation(u_hi[:, d, :], h[:, d, :], ACT.Copy, scale=gain).then_inc(h_hi_done, 1)
                    square_tile(c, Q_FFN + d, h[:, d, :])
                if not last:
                    load_x(c + 1)
                root_of(c, ST_FFN, None)
                act.preload_act_table_set(SILU_SET)
                up_phase(c, T_UP_A, U_UP_A, PART_A, 0)
                for d in range(KD):
                    split_to(c, U_DOWN_A + (d * PART_A) // 8 + 4)
                    done(c, T_DOWN_A + d)
                split_to(c, U_UP_B + 3)
                up_phase(c, T_UP_B, U_UP_B, PART_B, PART_A)
                act.preload_act_table_set(LN_EXP_SET)
                split_to(c, U_DOWN_B + 3)
                if not last:
                    norm_mix_with_splits(c)
                for d in range(KD):
                    split_to(c, min(U_DOWN_B + (d * PART_B) // 8 + 4, UNITS if last else UNITS + 3))
                    if d % 4 == 3:
                        act.wait_ge(out_ready, c * KD + (d + 1))
                        lo = d - 3
                        act.dma_start(out[bass.ds(c, 1), :, lo * T:(lo + 4) * T].rearrange("a p n -> p (a n)"),
                                      h[:, lo:lo + 4, :].rearrange("p k t -> p (k t)")).then_inc(out_stored, 16)
                if not last:
                    split_to(c, UNITS + 3)

            def square_tile(c, n, tile):
                if not (isinstance(c, int) and c == 0 and n < 2):
                    act.wait_ge(square_added, c * SQUARES + (n - 1))
                act.activation(square[:, n % 2, :], tile, ACT.Square).then_inc(square_ready, 1)

            def norm_mix_with_splits(c):
                nxt = c + 1
                act.wait_ge(x_loaded, nxt * 16)
                for k in range(KD):
                    square_tile(nxt, Q_MIX + k, x_in[:, k, :])
                split_to(c, U_DOWN_B + 6)
                root_of(nxt, ST_MIX, (g_ready, nxt * FT))
                for k in range(KD):
                    if k % 2 == 0:
                        split_to(c, U_DOWN_B + -(-(3 + k // 2) * PART_B // 8) + 2)
                    round_tile(nxt, N_MIX + k, u_hi[:, k, :])

            act.preload_act_table_set(LN_EXP_SET)
            act.wait_ge(consts, 2)
            for k in range(KD):
                if k % (KD // 2) == 0:
                    act.wait_ge(first_loaded[k // (KD // 2)], 16)
                square_tile(0, Q_MIX + k, x_in[:, k, :])
                if k == KD - 2:
                    act.wait_ge(rows_done, 1)
                    for n in range(2):
                        heads_of = slice(n * N_HEADS // 2, (n + 1) * N_HEADS // 2)
                        act.activation(rows[:, heads_of, :], psum[:, heads_of, 0:REL], ACT.Copy) \
                           .then_inc(rows_copied, 1)
            split_one(0, 16, None)
            root_of(0, ST_MIX, None)
            for k in range(KD):
                round_tile(0, N_MIX + k, u_hi[:, k, :])
                if k in (1, 5):
                    u = 1 + k // 4
                    split_one(u, 16 * (u // RAW_SLOTS + 1), None)
            with act.Fori(0, CHUNKS - 1) as c:
                chunk(c, False)
            chunk(CHUNKS - 1, True)
            act.wait_ge(out_stored, CHUNKS * 2 * 16 + 1)

        @block.vector
        def _(dve):
            def add_squares(c, first, n):
                for t in range(n):
                    dve.wait_ge(square_ready, c * SQUARES + (first + t + 1))
                    add_square(first + t, t)

            def add_square(n, t):
                if t == 0:
                    dve.tensor_copy(square_sum[:, :], square[:, n % 2, :]).then_inc(square_added, 1)
                else:
                    dve.tensor_tensor(square_sum[:, :], square_sum[:, :], square[:, n % 2, :], ALU.add) \
                       .then_inc(square_added, 1)
                dve.drain()

            def scale_tile(c, n, tile, gain):
                return dve.scalar_tensor_tensor(normed[:, n % 2, :], tile, vec[:, gain:gain + 1], rstd[:, :],
                                                ALU.mult, ALU.mult).then_inc(normed_ready, 1)

            def rest_of(c, n, hi, lo):
                dve.wait_ge(hi_done, c * NORMED + (n + 1))
                dve.tensor_tensor(lo, normed[:, n % 2, :], hi.bitcast(F32), ALU.subtract).then_inc(lo_done, 1)

            def normalise(c, first, tiles, gain0, his, los):
                for t, tile in enumerate(tiles):
                    scale_tile(c, first + t, tile, gain0 + t)
                    if t >= 1:
                        rest_of(c, first + t - 1, his[t - 1], los[t - 1])
                        dve.drain()
                rest_of(c, first + len(tiles) - 1, his[-1], los[-1])
                dve.drain()

            def norm_mix(c):
                add_squares(c, Q_MIX, KD)
                dve.wait_ge(rstd_ready, c * STATS + (ST_MIX + 1))
                normalise(c, N_MIX, [x_in[:, k, :] for k in range(KD)], V_MIX_G,
                          [u_hi[:, k, :] for k in range(KD)], [u_lo[:, k, :] for k in range(KD)])

            def norm_mix_beside_down(c):
                nxt = c + 1
                add_squares(nxt, Q_MIX, KD)
                for d in range(3):
                    add_to_h(c, T_DOWN_B, d, out_ready)
                dve.wait_ge(rstd_ready, nxt * STATS + (ST_MIX + 1))
                for d in range(3, KD):
                    ks = range(2 * (d - 3), min(2 * (d - 2), KD))
                    if ks:
                        normalise(nxt, N_MIX + ks[0], [x_in[:, k, :] for k in ks], V_MIX_G + ks[0],
                                  [u_hi[:, k, :] for k in ks], [u_lo[:, k, :] for k in ks])
                    add_to_h(c, T_DOWN_B, d, out_ready)

            def norm_qk(c, n, tile, gain, hi, lo):
                dve.wait_ge(rstd_ready, c * STATS + (ST_K + n + 1))
                scale_tile(c, N_K + n, psum[:, bank_of(tile), :], gain)
                dve.drain()
                dve.sem_inc(bank_free[bank_of(tile)], 1)
                rest_of(c, N_K + n, hi, lo)
                dve.drain()

            def softmax(c, m):
                hf = m % 2
                at = slice(4 * hf, 4 * hf + 4)
                dve.wait_ge(scores_done, c * HALVES + (m + 1))
                if m == 0:
                    dve.wait_ge(bias_loaded, 16)
                dve.scalar_tensor_tensor(scores.rearrange("p n k -> p (n k)"),
                                         psum[:, S_BANK:S_BANK + 2, :].rearrange("p n k -> p (n k)"),
                                         HEAD_DIM ** -0.5, bias[:, at, :].rearrange("p n k -> p (n k)"),
                                         ALU.mult, ALU.add)
                dve.drain()
                if m < 2:
                    dve.tensor_scalar(scores[:, :, 0:P], scores[:, :, 0:P], edge[:, :], None, ALU.add)
                    dve.drain()
                dve.tensor_reduce(top[:, at], scores, AXIS_X, ALU.max)
                dve.drain()
                sinks = vec[:, V_SINKS + 4 * hf:V_SINKS + 4 * hf + 4]
                dve.scalar_tensor_tensor(neg_top[:, at], top[:, at], -1.0, neg_sinks[:, at], ALU.mult, ALU.min) \
                   .then_inc(top_ready, 1)
                dve.drain()
                dve.tensor_tensor(sink_less[:, at], sinks, neg_top[:, at], ALU.add).then_inc(sink_ready, 1)
                if m == 1:
                    dve.memset(edge[:, :], 0.0)

            def divide_heads(c, i):
                dve.wait_ge(exp_done, c * HALVES + (2 * i + 2))
                total = denom[:, i % 2, :]
                dve.tensor_tensor(total, total, sink_exp[:, i % 2, :], ALU.add)
                dve.drain()
                dve.reciprocal(total, total)
                dve.drain()
                dve.wait_ge(pv_done, c * HALVES + (2 * i + 2))
                if i >= 1:
                    dve.wait_ge(heads_squared, c * BLOCKS + i)
                    dve.wait_ge(heads_turned, c * BLOCKS + i)
                dve.tensor_tensor(heads.rearrange("p (n d) -> p n d", n=N_HEADS),
                                  psum[:, STAT_BANK, :].rearrange("p (n d) -> p n d", n=N_HEADS),
                                  total.rearrange("p (n o) -> p n o", o=1).broadcast_to([P, N_HEADS, HEAD_DIM]),
                                  ALU.mult).then_inc(heads_ready, 1)

            def conv_taps(c, j):
                dve.wait_ge(tap_done, c * CT + (j + 1))
                for k in (1, 0):
                    w = V_CONV_W + 3 * j + k
                    dve.scalar_tensor_tensor(conv, gated[:, j, k:k + T], vec[:, w:w + 1], conv, ALU.mult, ALU.add)
                    dve.drain()
                dve.tensor_copy(gated[:, j, 0:2], gated[:, j, T:T + 2])

            def up_tile(c, i, done, n, f):
                gv = n % 2
                dve.wait_ge(pe_done, done)
                dve.tensor_tensor(up[:, gv, 2:2 + T], psum[:, n, :], rstd[:, :], ALU.mult).then_inc(bank_free[n], 1)
                tail = up_tail[:, bass.ds(f, 1), gv, :].rearrange("p a t -> p (a t)")
                dve.tensor_copy(up[:, gv, 0:2], tail)
                dve.drain()
                w = [vec[:, bass.ds(f * 8 + (V_FFN + gv * 4 + k), 1)] for k in range(4)]
                dve.tensor_scalar(up_conv[:, gv, :], up[:, gv, 2:2 + T], w[2], w[3], ALU.mult, ALU.add)
                dve.tensor_copy(tail, up[:, gv, T:T + 2])
                dve.drain()
                dve.scalar_tensor_tensor(up_conv[:, gv, :], up[:, gv, 1:1 + T], w[1], up_conv[:, gv, :],
                                         ALU.mult, ALU.add)
                dve.drain()
                return dve.scalar_tensor_tensor(up_conv[:, gv, :], up[:, gv, 0:T], w[0], up_conv[:, gv, :],
                                                ALU.mult, ALU.add)

            def up_phase(c, tile0, part, f0):
                with dve.Fori(0, part // 2) as i:
                    for e in range(2):
                        f = i * 2 + (f0 + e)
                        pair = c * FT + f
                        n = 2 * e
                        if tile0 == T_UP_A and e == 0:
                            dve.wait_ge(rstd_ready, c * STATS + (ST_FFN + 1))
                        up_tile(c, i, c * EVENTS + i * 4 + (tile_end(tile0 + n) + 1), n, f).then_inc(gate_ready, 1)
                        up_tile(c, i, c * EVENTS + i * 4 + (tile_end(tile0 + n + 1) + 1), n + 1, f)
                        dve.drain()
                        dve.wait_ge(silu_done, pair + 1)
                        dve.tensor_tensor(product32, up_conv[:, 0, :], up_conv[:, 1, :], ALU.mult) \
                           .then_inc(product_ready, 1)
                        dve.wait_ge(g_hi_done, pair + 1)
                        gh, gl = (g[:, bass.ds(i * 2 + e, 1), :].rearrange("p a t -> p (a t)") for g in (g_hi, g_lo))
                        dve.tensor_tensor(gl, product32, gh.bitcast(F32), ALU.subtract).then_inc(g_ready, 1)
                        dve.drain()

            def add_to_h(c, tile0, d, ready=None):
                dve.wait_ge(pe_done, c * EVENTS + (tile_end(tile0 + d) + 1))
                bank = bank_of(tile0 + d)
                dve.tensor_tensor(h[:, d, :], psum[:, bank, :], h[:, d, :], ALU.add).then_inc(bank_free[bank], 1)
                dve.drain()
                if ready is not None:
                    dve.sem_inc(ready, 1)

            def out_tile(c, d):
                dve.wait_ge(pe_done, c * EVENTS + (tile_end(T_OUT + d) + 1))
                part = normed[:, d % 2, :]
                banks = [bank_of(T_OUT + d, n) for n in range(2)]
                dve.tensor_tensor(part, psum[:, banks[0], :], rstd[:, :], ALU.mult).then_inc(bank_free[banks[0]], 1)
                dve.tensor_tensor(h[:, d, :], psum[:, banks[1], :], rstd_attn[:, :], ALU.mult) \
                   .then_inc(bank_free[banks[1]], 1)
                dve.drain()
                dve.tensor_tensor(part, part, x_in[:, d, :], ALU.add)
                dve.drain()
                dve.tensor_tensor(h[:, d, :], h[:, d, :], part, ALU.add).then_inc(h_ready, 1)

            def split_h(c, d):
                dve.wait_ge(h_hi_done, c * KD + (d + 1))
                gain = vec[:, V_FFN_G + d:V_FFN_G + d + 1]
                dve.scalar_tensor_tensor(u_lo[:, d, :], h[:, d, :], gain, u_hi[:, d, :].bitcast(F32),
                                         ALU.mult, ALU.subtract).then_inc(h_split, 1)
                dve.wait_ge(square_ready, c * SQUARES + (Q_FFN + d + 1))
                add_square(Q_FFN + d, d)

            def chunk(c, last):
                for k in (k_hi, k_lo):
                    dve.tensor_copy(k[:, 0:P], k[:, T:T + P].bitcast(F32))
                dve.tensor_copy(v_sb[:, 0, :], v_sb[:, BLOCKS, :])
                dve.drain()
                dve.sem_inc(tails_moved, 1)
                dve.wait_ge(v_copied, c + 1)
                dve.sem_inc(bank_free[bank_of(U_V)], 1)
                norm_qk(c, 0, U_K, V_K_G, k_hi[:, P:P + T], k_lo[:, P:P + T])
                for p in range(QT):
                    norm_qk(c, 1 + p, U_Q + p, V_Q_G, g_hi[:, KD + p, :], g_lo[:, KD + p, :])
                for m in range(-1, 3 * CT - 1):
                    n = m + 1
                    j, kind = n // 3, n % 3
                    tile = U_CONV + n
                    if kind == 0:
                        dve.wait_ge(c_copied, c * CT + (j + 1))
                        dve.sem_inc(bank_free[bank_of(tile)], 1)
                    elif kind == 1:
                        dve.wait_ge(pe_done, c * EVENTS + (tile_end(tile) + 1))
                        dve.tensor_tensor(gated[:, j, 2:2 + T], psum[:, bank_of(tile), :], gate_c, ALU.mult) \
                           .then_inc(gated_ready, 1)
                        dve.drain()
                        dve.sem_inc(bank_free[bank_of(tile)], 1)
                    else:
                        dve.wait_ge(pe_done, c * EVENTS + (tile_end(tile) + 1))
                        dve.tensor_tensor(normed[:, j % 2, :], psum[:, bank_of(tile), :], conv, ALU.mult) \
                           .then_inc(y_ready, 1)
                        dve.drain()
                        dve.sem_inc(bank_free[bank_of(tile)], 1)
                    if m < 0:
                        continue
                    if 2 <= m < HALVES + 2 and m % 2 == 1:
                        divide_heads(c, (m - 3) // 2)
                    if 1 <= m < HALVES + 1:
                        dve.wait_ge(turned, c * 2 * HALVES + (2 * m - 1))
                        dve.tensor_copy(probs_t[:, 0, :], psum[:, PT_BANKS[0], :]).then_inc(pt_first, 1)
                    if m < HALVES:
                        softmax(c, m)
                    if 2 <= m < HALVES + 2 and m % 2 == 1:
                        i = (m - 3) // 2
                        dve.wait_ge(heads_hi_done, c * BLOCKS + (i + 1))
                        for p in range(QT):
                            gain = vec[:, V_ATTN_G + p:V_ATTN_G + p + 1]
                            lo = dve.scalar_tensor_tensor(g_lo[:, CT + p, i * P:(i + 1) * P],
                                                          psum[:, PT_BANKS[0], p * P:(p + 1) * P], gain,
                                                          g_hi[:, CT + p, i * P:(i + 1) * P].bitcast(F32),
                                                          ALU.mult, ALU.subtract)
                        lo.then_inc(attn_split, 1)
                    if kind == 1:
                        conv_taps(c, j)
                    if kind == 2:
                        dve.wait_ge(y_hi_done, c * CT + (j + 1))
                        gain = vec[:, V_CONV_G + j:V_CONV_G + j + 1]
                        dve.scalar_tensor_tensor(g_lo[:, j, :], normed[:, j % 2, :], gain,
                                                 g_hi[:, j, :].bitcast(F32), ALU.mult, ALU.subtract) \
                           .then_inc(conv_split, 1)
                        dve.wait_ge(square_ready, c * SQUARES + (Q_CONV + j + 1))
                        add_square(Q_CONV + j, j)
                dve.wait_ge(rstd_ready, c * STATS + (ST_CONV + 1))
                dve.wait_ge(out_stored, c * 32 + 1)
                for d in range(KD):
                    out_tile(c, d)
                    if d >= 1:
                        split_h(c, d - 1)
                split_h(c, KD - 1)
                up_phase(c, T_UP_A, PART_A, 0)
                for d in range(KD):
                    add_to_h(c, T_DOWN_A, d)
                up_phase(c, T_UP_B, PART_B, PART_A)
                if last:
                    for d in range(KD):
                        add_to_h(c, T_DOWN_B, d, out_ready)
                else:
                    norm_mix_beside_down(c)

            dve.memset(mean_model, 1.0 / D_MODEL)
            dve.memset(mean_branch, 1.0 / CONV_WIDTH)
            dve.memset(edge[:, :], MASKED)
            dve.memset(eps[:, :], EPS)
            dve.memset(k_hi[:, T:T + P].bitcast(F32), 0.0)
            dve.memset(k_lo[:, T:T + P].bitcast(F32), 0.0)
            dve.memset(v_sb[:, BLOCKS, :], 0.0)
            dve.memset(up_tail[:, :, :, :], 0.0)
            dve.memset(gated[:, :, 0:2], 0.0)
            dve.drain()
            dve.sem_inc(pe_done, 1)
            dve.sem_inc(out_stored, 1)
            for b in range(BANKS):
                dve.sem_inc(bank_free[b], 1)
            dve.sem_inc(consts, 2)
            dve.wait_ge(vec_loaded, 64)
            dve.memset(table[NUM_BUCKETS:NUM_BUCKETS + 1, :], 1.0)
            dve.tensor_scalar(neg_sinks[:, :], vec[:, V_SINKS:V_SINKS + N_HEADS], -1.0, None, ALU.mult)
            dve.drain()
            dve.tensor_copy(table_wide, table[:, :].rearrange("p (n o) -> p n o", o=1)
                            .broadcast_to([NUM_BUCKETS + 1, N_HEADS, P])).then_inc(wide_ready, 1)
            norm_mix(0)
            with dve.Fori(0, CHUNKS - 1) as c:
                chunk(c, False)
            chunk(CHUNKS - 1, True)


def relative_buckets():
    a = np.zeros((NUM_BUCKETS + 1, REL), np.float32)
    for m in range(REL):
        d = 2 * P - 1 - m
        if 0 <= d < WINDOW:
            b = d
            if d >= MAX_EXACT:
                b = MAX_EXACT + int(math.log(d / MAX_EXACT) / math.log(MAX_DISTANCE / MAX_EXACT)
                                    * (NUM_BUCKETS - MAX_EXACT))
            a[min(b, NUM_BUCKETS - 1), m] = 1.0
        else:
            a[NUM_BUCKETS, m] = MASKED
    return a


def lay_out(a):
    a = {k: np.asarray(v) for k, v in a.items()}
    pairs = [n for p in range(QT) for n in (p, p + QT)]
    scored = [2 * f + n + QT * e for f in range(2) for e in range(2) for n in range(2)]
    x = a["x"][0].reshape(CHUNKS, T, KD, P).transpose(0, 3, 2, 1).reshape(CHUNKS, P, KD * T)

    def units(w, order):
        k, n = w.shape
        return w.reshape(k // P, P, n // P, P).transpose(2, 1, 0, 3)[order].reshape(len(order), P, k)

    w_in = a["w_in"][0]
    q0 = 3 * CONV_WIDTH
    q = w_in[:, q0:q0 + ATTN_WIDTH].reshape(D_MODEL, N_HEADS, HEAD_DIM)[:, pairs].reshape(D_MODEL, ATTN_WIDTH)
    w_in = np.concatenate([w_in[:, :q0], q, w_in[:, q0 + ATTN_WIDTH:]], axis=1)
    first = 3 * CT + QT
    order = [first, first + 1] + [3 * CT + p for p in range(QT)]
    for j in range(CT):
        order += [CT + j, 2 * CT + j, j]
    w_out = a["w_out"][0]
    w_attn = w_out[CONV_WIDTH:].reshape(N_HEADS, HEAD_DIM, D_MODEL)[scored].reshape(ATTN_WIDTH, D_MODEL)
    w_out = np.concatenate([w_out[:CONV_WIDTH], w_attn])
    w_up, w_down = a["w_up"][0], a["w_down"][0]

    def up(f0, n):
        return units(w_up, [g * FT + f for f in range(f0, f0 + n) for g in range(2)])

    def down(f0, n):
        w = w_down.reshape(FT, P, KD, P)[f0:f0 + n].transpose(2, 0, 1, 3).reshape(n * KD // 8, 8, P, P)
        return w.transpose(0, 2, 1, 3).reshape(n * KD // 8, P, 8 * P)

    weights = np.concatenate([units(w_in, order), units(w_out, list(range(KD))),
                              up(0, PART_A), down(0, PART_A), up(PART_A, PART_B), down(PART_A, PART_B)])

    def columns(v):
        return v.reshape(-1, P).T

    conv = a["conv_w"][0].reshape(3, CT, P).transpose(2, 1, 0).reshape(P, 3 * CT)
    taps = np.concatenate([a["ffn_conv_w"][0], a["ffn_conv_b"]]).reshape(4, 2, FT, P)
    attn_g = a["out_norm_attn_g"][0].reshape(N_HEADS, HEAD_DIM)[scored].reshape(-1)
    vectors = np.concatenate([
        columns(a["norm_mix_g"][0]), columns(a["norm_ffn_g"][0]), columns(a["out_norm_conv_g"][0]), columns(attn_g),
        columns(np.tile(a["q_norm_g"][0], 2)), columns(np.tile(a["k_norm_g"][0], 2)), conv,
        np.broadcast_to(a["sinks"][0][scored], (P, N_HEADS)),
        taps.transpose(3, 2, 1, 0).reshape(P, FT * 8)], axis=1)
    same_head = np.kron(np.eye(2), np.ones((HEAD_DIM, HEAD_DIM))) / HEAD_DIM
    fixed = np.concatenate([np.eye(P), same_head], axis=1).astype(np.float32)
    out = {"x": x, "weights": weights, "vectors": vectors, "rel_table": a["rel_bias_table"][:, scored],
           "fixed": fixed, "bucket_rows": relative_buckets()}
    return {k: np.ascontiguousarray(v) for k, v in out.items()}


def kernel(**inputs):
    import concourse.bacc as bacc
    from concourse.bass_utils import run_bass_kernel_spmd

    nc = bacc.Bacc("TRN2", target_bir_lowering=False, num_devices=1)
    arrays = lay_out(inputs)
    args = [nc.dram_tensor(n, a.shape, F32, kind="ExternalInput").ap() for n, a in arrays.items()]
    bias_rows = nc.dram_tensor("bias_rows", (N_HEADS, P, REL), F32, kind="Internal").ap()
    out = nc.dram_tensor("out", (CHUNKS, P, KD * T), F32, kind="ExternalOutput").ap()
    build_layer(nc, *args, bias_rows, out)
    result = run_bass_kernel_spmd(nc, [arrays], core_ids=[0]).results[0]["out"]
    return result.reshape(CHUNKS, P, KD, T).transpose(0, 3, 2, 1).reshape(1, SEQ, D_MODEL)
```

```python
import math
from contextlib import ExitStack

import numpy as np

import concourse.bass as bass
from concourse import mybir

F32 = mybir.dt.float32
F32R = mybir.dt.float32r
ACT = mybir.ActivationFunctionType
ALU = mybir.AluOpType
LN_EXP_SET, SILU_SET = "natural_log_exp_and_others", "silu_and_others"
AXIS_X = mybir.AxisListType.X

P = 128
D_MODEL, SEQ = 1024, 2048
CONV_WIDTH, ATTN_WIDTH, HEAD_DIM, N_HEADS, N_KV = 512, 512, 64, 8, 2
D_FF = 2816
NUM_BUCKETS, MAX_DISTANCE, WINDOW = 32, 128, 128
MAX_EXACT = NUM_BUCKETS // 2
EPS = 1e-6
MASKED = -1e30

T = 512
CHUNKS = SEQ // T
KD = D_MODEL // P
QT = N_HEADS // 2
CT = CONV_WIDTH // P
BLOCKS = T // P
HALVES = 2 * BLOCKS
FT = D_FF // P
PART_A, PART_B = 12, 10
SLOTS = 4
RAW_SLOTS = 2

U_K, U_V, U_Q, U_CONV = 0, 1, 2, 2 + QT
U_OUT = U_CONV + 3 * CT
U_UP_A = U_OUT + KD
U_DOWN_A = U_UP_A + 2 * PART_A
U_UP_B = U_DOWN_A + PART_A * KD // 8
U_DOWN_B = U_UP_B + 2 * PART_B
UNITS = U_DOWN_B + PART_B * KD // 8

T_OUT = U_OUT
T_UP_A = T_OUT + KD
T_DOWN_A = T_UP_A + 2 * PART_A
T_UP_B = T_DOWN_A + KD
T_DOWN_B = T_UP_B + 2 * PART_B
TILES = T_DOWN_B + KD

DOWN_ENDS = {n: sorted({k for k in range(1, n * KD + 1) if k % 8 == 0 or k % n == 0}) for n in (PART_A, PART_B)}
E_DOWN_A = U_DOWN_A
E_UP_B = E_DOWN_A + len(DOWN_ENDS[PART_A])
E_DOWN_B = E_UP_B + 2 * PART_B
EVENTS = E_DOWN_B + len(DOWN_ENDS[PART_B])


def unit_end(u):
    for unit0, event0, part in ((U_DOWN_B, E_DOWN_B, PART_B), (U_DOWN_A, E_DOWN_A, PART_A)):
        if unit0 <= u < unit0 + part * KD // 8:
            return event0 + DOWN_ENDS[part].index(8 * (u - unit0 + 1)) + 1
    return (u + 1) if u < U_DOWN_A else E_UP_B + (u - U_UP_B) + 1


def tile_end(t):
    for tile0, event0, part in ((T_DOWN_B, E_DOWN_B, PART_B), (T_DOWN_A, E_DOWN_A, PART_A)):
        if tile0 <= t < tile0 + KD:
            return event0 + DOWN_ENDS[part].index(part * (t - tile0 + 1)) + 1
    return (t + 1) if t < T_DOWN_A else E_UP_B + (t - T_UP_B) + 1


ST_MIX, ST_K, ST_Q, ST_ATTN, ST_CONV, ST_FFN = 0, 1, 2, 2 + QT, 3 + QT, 4 + QT
STATS = 5 + QT
N_MIX, N_K, N_Q = 0, KD, KD + 1
NORMED = N_Q + QT
Q_MIX, Q_CONV = 0, KD
Q_FFN = Q_CONV + CT
SQUARES = Q_FFN + KD
BANK_USES = ([(t, 0, t) for t in range(U_CONV)] + [(t, 0, t % 3) for t in range(U_CONV, T_OUT)]
             + [(T_OUT + d, part, 3 * part + d % 3) for d in range(KD) for part in range(2)]
             + [(t, 0, (t - first) % 4) for first, end in
                ((T_UP_A, T_DOWN_A), (T_DOWN_A, T_UP_B), (T_UP_B, T_DOWN_B), (T_DOWN_B, TILES))
                for t in range(first, end)])
BANKS = 6
USES = [sum(bank == b for _, _, bank in BANK_USES) for b in range(BANKS)]


def bank_of(tile, part=0):
    return next(b for t, p, b in BANK_USES if (t, p) == (tile, part))


def uses_before(tile, part=0):
    at = next(n for n, (t, p, _) in enumerate(BANK_USES) if (t, p) == (tile, part))
    return sum(b == bank_of(tile, part) for _, _, b in BANK_USES[:at])


V_MIX_G, V_FFN_G = 0, KD
V_CONV_G = 2 * KD
V_ATTN_G = V_CONV_G + CT
V_Q_G = V_ATTN_G + QT
V_K_G = V_Q_G + 1
V_CONV_W = V_K_G + 1
V_SINKS = V_CONV_W + 3 * CT
V_FFN = V_SINKS + N_HEADS
V_COLS = V_FFN + FT * 2 * 4
DVE_HEADS = 1
REL = 3 * P


def build_layer(nc, x, weights, vectors, rel_table, fixed, bucket_rows, bias_rows, out):
    ctx = ExitStack()
    with ctx:
        def sb(name, shape, dt=F32):
            return ctx.enter_context(nc.sbuf_tensor(name, shape, dt))

        def sem(name):
            return ctx.enter_context(nc.semaphore(name))

        w_raw = sb("w_raw", [P, RAW_SLOTS, KD * P])
        w_hi = sb("w_hi", [P, SLOTS, KD * P], F32R)
        w_lo = sb("w_lo", [P, SLOTS, KD * P], F32R)
        x_in = sb("x_in", [P, KD, T])
        h = sb("h", [P, KD, T])
        u_hi = sb("u_hi", [P, KD, T], F32R)
        u_lo = sb("u_lo", [P, KD, T], F32R)
        g_hi = sb("g_hi", [P, PART_A, T], F32R)
        g_lo = sb("g_lo", [P, PART_A, T], F32R)
        k_hi = sb("k_hi", [P, P + T], F32R)
        k_lo = sb("k_lo", [P, P + T], F32R)
        v_before_hi = sb("v_before_hi", [P, 1, 2, P], F32R)
        v_before_lo = sb("v_before_lo", [P, 1, 2, P], F32R)
        gated = sb("gated", [P, CT, 2 + T])
        up_tail = sb("up_tail", [P, FT, 2, 2])
        square = sb("square", [P, 2, T])
        square_sum = sb("square_sum", [P, T])
        rstd = sb("rstd", [P, T])
        rstd_attn = sb("rstd_attn", [P, T])
        normed = sb("normed", [P, 2, T])
        shared = sb("shared", [P, 5 * T + 4])
        head_square = sb("head_square", [P, 2, P])
        gate_c = shared[:, 3 * T:4 * T]
        conv = shared[:, 4 * T:5 * T]
        v_t = conv
        scores = h[:, 0:4, :].rearrange("p k t -> p (k t)").rearrange("p (b n k) -> p b n k", b=2, n=4)
        probs_hi, probs_lo = g_hi[:, CT:CT + 2, :], g_lo[:, CT:CT + 2, :]
        v_hi, v_lo = (g[:, CT + 2:CT + 4, :].rearrange("p k t -> p (k t)")
                       .rearrange("p (b e d) -> p b e d", b=BLOCKS, e=2) for g in (g_hi, g_lo))
        up_conv = shared[:, 0:2 * T].rearrange("p (n t) -> p n t", n=2)
        product32 = shared[:, 2 * T:3 * T]
        up = shared[:, 3 * T:5 * T + 4].rearrange("p (n t) -> p n t", n=2)
        bias = sb("bias", [P, N_HEADS, 2 * P])
        vec = sb("vec", [P, V_COLS])
        table = sb("table", [NUM_BUCKETS + 1, N_HEADS])
        fix = sb("fix", [P, 2, P])
        mean_model = sb("mean_model", [P, P])[:, :]
        mean_branch = sb("mean_branch", [P, P])[:, :]
        edge = sb("edge", [P, 1])
        eps = sb("eps", [P, 1])
        top = sb("top", [P, N_HEADS])
        neg_sinks = sb("neg_sinks", [P, N_HEADS])
        neg_top = sb("neg_top", [P, N_HEADS])
        sink_less = sb("sink_less", [P, N_HEADS])
        sink_exp = sb("sink_exp", [P, 2, N_HEADS])
        denom = sb("denom", [P, 2, N_HEADS])
        identity, mean_head = fix[:, 0, :], fix[:, 1, :]
        table_wide = shared[0:NUM_BUCKETS + 1, 0:N_HEADS * P].rearrange("p (n k) -> p n k", n=N_HEADS)
        buckets = shared[0:NUM_BUCKETS + 1, 2 * T:2 * T + REL]
        rows = h[:, 0:REL * N_HEADS // T, :].rearrange("p k t -> p (k t)").rearrange("p (n m) -> p n m", n=N_HEADS)

        psum = ctx.enter_context(nc.psum_tensor("psum", [P, 8, T], F32))
        S_BANK, PT_BANKS, STAT_BANK = 4, (6, 3), 7

        w_loaded = [sem(f"w_loaded{s}") for s in range(RAW_SLOTS)]
        w_hi_done, w_ready = sem("w_hi_done"), sem("w_ready")
        pe_done = sem("pe_done")
        bank_free = [sem(f"bank_free{b}") for b in range(BANKS)]
        stat_done, stat_read, rstd_ready = sem("stat_done"), sem("stat_read"), sem("rstd_ready")
        qk_square = sem("qk_square")
        square_ready, square_added = sem("square_ready"), sem("square_added")
        normed_ready, hi_done, lo_done = sem("normed_ready"), sem("hi_done"), sem("lo_done")
        v_copied, v_turned, v_hi_done = sem("v_copied"), sem("v_turned"), sem("v_hi_done")
        v_split, tails_moved = sem("v_split"), sem("tails_moved")
        scores_done, scores_read = sem("scores_done"), sem("scores_read")
        top_ready, exp_done = sem("top_ready"), sem("exp_done")
        share_ready, probs_shared = sem("share_ready"), sem("probs_shared")
        probs_ready, turned = sem("probs_ready"), sem("turned")
        probs_hi_done, probs_split = sem("probs_hi_done"), sem("probs_split")
        pv_done, attn_split = sem("pv_done"), sem("attn_split")
        heads_squared, heads_summed = sem("heads_squared"), sem("heads_summed")
        c_copied, gated_ready, tap_done, y_ready = sem("c_copied"), sem("gated_ready"), sem("tap_done"), sem("y_ready")
        y_hi_done, conv_split = sem("y_hi_done"), sem("conv_split")
        h_ready, h_hi_done, h_split = sem("h_ready"), sem("h_hi_done"), sem("h_split")
        gate_ready, silu_done = sem("gate_ready"), sem("silu_done")
        product_ready, g_hi_done, g_ready = sem("product_ready"), sem("g_hi_done"), sem("g_ready")
        first_loaded = [sem(f"first_loaded{n}") for n in range(2)]
        x_loaded, out_ready, out_stored = sem("x_loaded"), sem("out_ready"), sem("out_stored")
        consts, vec_loaded = sem("consts"), sem("vec_loaded")
        wide_ready, rows_done = sem("wide_ready"), sem("rows_done")
        first_rows_copied, last_rows_copied = sem("first_rows_copied"), sem("last_rows_copied")
        rows_stored, bias_loaded = sem("rows_stored"), sem("bias_loaded")
        sink_ready = sem("sink_ready")

        block = ctx.enter_context(nc.Block())

        @block.sync
        def _(sp):
            def load(unit, slot):
                sp.dma_start(w_raw[:, slot, :], weights[bass.ds(unit, 1), :, :].rearrange("a p n -> p (a n)")) \
                  .then_inc(w_loaded[slot], 16)

            sp.dma_start(table[0:NUM_BUCKETS, :], rel_table).then_inc(vec_loaded, 16)
            sp.dma_start(buckets, bucket_rows).then_inc(vec_loaded, 16)
            sp.dma_start(vec[:, :], vectors).then_inc(vec_loaded, 16)
            sp.dma_start(fix[:, :, :], fixed.rearrange("p (n k) -> p n k", n=2)).then_inc(vec_loaded, 16)
            for n in range(2):
                half = slice(n * KD // 2, (n + 1) * KD // 2)
                sp.dma_start(x_in[:, half, :],
                             x[0:1, :, half.start * T:half.stop * T].rearrange("a p (k t) -> p (a k) t", t=T)) \
                  .then_inc(first_loaded[n], 16)
            for s in range(RAW_SLOTS):
                load(s, s)
            sp.wait_ge(first_rows_copied, 1)
            sp.wait_ge(last_rows_copied, 1)
            sp.dma_start(bias_rows.rearrange("n q m -> q n m"), rows).then_inc(rows_stored, 16)
            for s in range(RAW_SLOTS):
                sp.wait_ge(w_ready, s + 1)
                load(RAW_SLOTS + s, s)
            sp.wait_ge(rows_stored, 16)
            skewed = bias_rows.rearrange("n q m -> n (q m)")[:, P - 1:P - 1 + P * (REL - 1)] \
                              .rearrange("n (q m) -> q n m", m=REL - 1)[:, :, 0:2 * P]
            sp.dma_start(bias[:, :, :], skewed).then_inc(bias_loaded, 16)
            with sp.Fori(2, UNITS // RAW_SLOTS) as i:
                for s in range(RAW_SLOTS):
                    unit = sp.snap(i * RAW_SLOTS + s)
                    sp.wait_ge(w_ready, i * RAW_SLOTS + (s + 1 - RAW_SLOTS))
                    load(unit, s)
            with sp.Fori(1, CHUNKS) as c:
                with sp.Fori(0, UNITS // RAW_SLOTS) as i:
                    for s in range(RAW_SLOTS):
                        unit = sp.snap(i * RAW_SLOTS + s)
                        sp.wait_ge(w_ready, c * UNITS + i * RAW_SLOTS + (s + 1 - RAW_SLOTS))
                        load(unit, s)

        @block.gpsimd
        def _(pool):
            with pool.Fori(0, CHUNKS * UNITS // SLOTS) as i:
                for s in range(SLOTS):
                    pool.wait_ge(w_hi_done, i * SLOTS + (s + 1))
                    pool.tensor_tensor(w_lo[:, s, :], w_raw[:, s % RAW_SLOTS, :], w_hi[:, s, :].bitcast(F32),
                                       ALU.subtract).then_inc(w_ready, 1)

        @block.tensor
        def _(pe):
            def product(bank, free, pairs, middle=None, event=True, at=None):
                pe.wait_ge(bank_free[bank], free)
                seen = None
                for n, (unit, name, k, last_use, a_hi, a_lo, waits) in enumerate(pairs):
                    if name != seen:
                        pe.wait_ge(w_ready, unit + 1)
                        seen = name
                    for s, v in waits:
                        pe.wait_ge(s, v)
                    slot = name % SLOTS
                    hi, lo = w_hi[:, slot, k * P:(k + 1) * P], w_lo[:, slot, k * P:(k + 1) * P]
                    end = n == len(pairs) - 1
                    pe.matmul(psum[:, bank, :], hi, a_hi, start=n == 0, stop=False)
                    pe.matmul(psum[:, bank, :], hi, a_lo, start=False, stop=False)
                    mm = pe.matmul(psum[:, bank, :], lo, a_hi, start=False, stop=end)
                    if last_use or (end and event):
                        mm.then_inc(pe_done, 1)
                    if middle and n == (at or len(pairs) // 2) - 1:
                        middle()

            def projection(c, tile, unit, name, a_hi, a_lo, first=None, middle=None, free=None, bank=None, at=None):
                pairs = [(unit, name, k, k == KD - 1, a_hi[:, k, :], a_lo[:, k, :],
                          [(first[0], first[1] + k + 1)] if first is not None else []) for k in range(KD)]
                bank = bank_of(tile) if bank is None else bank
                free = c * USES[bank] + (uses_before(tile) + 1) if free is None else free
                product(bank, free, pairs, middle, at=at)

            def branch_part(c, d, part, ends):
                tile, u = T_OUT + d, U_OUT + d
                split, each = ((conv_split, CT), (attn_split, HALVES))[part]
                ks = range(part * CT, (part + 1) * CT)
                first = (0, KD)[part]
                pairs = [(c * UNITS + u, u, k, False, g_hi[:, first + k % CT, :], g_lo[:, first + k % CT, :],
                          [] if d else [(split, c * each + (k % CT + 1 if part == 0 else each))]) for k in ks]
                bank = bank_of(tile, part)
                product(bank, c * USES[bank] + (uses_before(tile, part) + 1), pairs, event=ends)

            def statistic(c, index, ready, value, mean, squares):
                pe.wait_ge(ready, value)
                if not (isinstance(c, int) and c == 0 and index == 0):
                    pe.wait_ge(stat_read, c * STATS + index)
                pe.matmul(psum[:, STAT_BANK, :], mean, squares, start=True, stop=True).then_inc(stat_done, 1)

            def qk_statistic(c, n):
                statistic(c, ST_K + n, qk_square, c * (1 + QT) + (n + 1), mean_head, square[:, 0, :])

            def turn_v(c):
                pe.wait_ge(v_copied, c + 1)
                for b in range(BLOCKS):
                    mm = pe.transpose(psum[:, PT_BANKS[0], b * P:(b + 1) * P], v_t[:, b * P:(b + 1) * P], identity)
                mm.then_inc(v_turned, 1)

            def score(c, m):
                i, hf = m // 2, m % 2
                if m == 0:
                    pe.wait_ge(lo_done, c * NORMED + NORMED)
                    for b in (S_BANK, S_BANK + 1):
                        pe.wait_ge(bank_free[b], c * USES[b] + (uses_before(T_OUT + b - 3, 1) + 1))
                else:
                    pe.wait_ge(scores_read, c * HALVES + m)
                for n in range(2):
                    p = 2 * hf + n
                    for e in range(2):
                        rows = slice(e * HEAD_DIM, (e + 1) * HEAD_DIM)
                        o = psum[:, S_BANK + e, n * 2 * P:(n + 1) * 2 * P]
                        qh, ql = (g[rows, KD + p, i * P:(i + 1) * P] for g in (g_hi, g_lo))
                        kh, kl = (k[rows, i * P:(i + 2) * P] for k in (k_hi, k_lo))
                        pe.matmul(o, qh, kh, start=True, stop=False)
                        pe.matmul(o, qh, kl, start=False, stop=False)
                        mm = pe.matmul(o, ql, kh, start=False, stop=True)
                mm.then_inc(scores_done, 1)

            def turn_probs(c, m):
                pe.wait_ge(probs_ready, c * HALVES + (m + 1))
                pe.wait_ge(probs_shared, c * HALVES + (m + 1))
                if m == 0:
                    pe.wait_ge(v_split, c + 1)
                    pe.wait_ge(bank_free[3], c * USES[3] + (uses_before(T_OUT, 1) + 1))
                else:
                    pe.wait_ge(probs_split, c * HALVES + m)
                for e in range(2):
                    for n in range(2):
                        for kt in range(2):
                            at = 2 * kt + n
                            mm = pe.transpose(psum[:, PT_BANKS[e], at * P:(at + 1) * P],
                                              scores[:, m % 2, 2 * e + n, kt * P:(kt + 1) * P], identity)
                    mm.then_inc(turned, 1)

            def weigh_values(c, m):
                i = m // 2
                pe.wait_ge(probs_split, c * HALVES + (m + 1))
                if m == 0:
                    pe.wait_ge(stat_read, c * STATS + ST_ATTN)
                else:
                    pe.wait_ge(attn_split, c * HALVES + m)
                o = psum[:, STAT_BANK, 0:2 * P]
                for e in range(2):
                    for kt in range(2):
                        vh, vl = (v_before_hi[:, 0, e, :], v_before_lo[:, 0, e, :]) if i + kt == 0 else \
                                 (v_hi[:, i + kt - 1, e, :], v_lo[:, i + kt - 1, e, :])
                        ph, pl = (probs[:, e, kt * 2 * P:(kt + 1) * 2 * P] for probs in (probs_hi, probs_lo))
                        pe.matmul(o, vh, ph, start=(e, kt) == (0, 0), stop=False)
                        pe.matmul(o, vh, pl, start=False, stop=False)
                        mm = pe.matmul(o, vl, ph, start=False, stop=(e, kt) == (1, 1))
                mm.then_inc(pv_done, 1)

            def attention_step(c, m):
                if m >= 3:
                    weigh_values(c, m - 3)
                if 2 <= m < HALVES + 2:
                    turn_probs(c, m - 2)
                if m < HALVES:
                    score(c, m)

            def up_projection(c, tile0, unit0, part, start=0):
                with pe.Fori(start, part // 2) as i:
                    for n in range(4):
                        projection(c, tile0 + n, c * UNITS + i * 4 + (unit0 + n), unit0 + n, u_hi, u_lo,
                                   free=c * USES[n] + i + (uses_before(tile0 + n) + 1), bank=n)

            def down_projection(c, tile0, unit0, part, g0, middle=None):
                for d in range(KD):
                    pairs = []
                    for k in range(part):
                        at = d * part + k
                        pairs.append((c * UNITS + (unit0 + at // 8), unit0 + at // 8, at % 8,
                                      at % 8 == 7, g_hi[:, k, :], g_lo[:, k, :],
                                      [(g_ready, c * FT + (g0 + k + 1))] if d == 0 else []))
                    bank = bank_of(tile0 + d)
                    product(bank, c * USES[bank] + (uses_before(tile0 + d) + 1), pairs,
                            middle if d == 2 else None)

            def chunk(c, last):
                def unit(n):
                    return c * UNITS + n

                projection(c, U_K, unit(U_K), U_K, u_hi, u_lo, first=(lo_done, c * NORMED + N_MIX))
                projection(c, U_V, unit(U_V), U_V, u_hi, u_lo, middle=lambda: qk_statistic(c, 0))
                projection(c, U_Q, unit(U_Q), U_Q, u_hi, u_lo, middle=lambda: turn_v(c))
                for p in range(1, QT):
                    projection(c, U_Q + p, unit(U_Q + p), U_Q + p, u_hi, u_lo,
                               middle=lambda p=p: qk_statistic(c, p))
                projection(c, U_CONV, unit(U_CONV), U_CONV, u_hi, u_lo, middle=lambda: qk_statistic(c, QT))
                for m in range(3 * CT - 1):
                    if m < 3 * CT - 2:
                        projection(c, U_CONV + 1 + m, unit(U_CONV + 1 + m), U_CONV + 1 + m, u_hi, u_lo)
                        attention_step(c, m)
                    else:
                        projection(c, U_CONV + 1 + m, unit(U_CONV + 1 + m), U_CONV + 1 + m, u_hi, u_lo,
                                   middle=lambda: attention_step(c, m), at=KD - 2)
                branch_part(c, 0, 1, False)
                statistic(c, ST_ATTN, heads_summed, c * HALVES + HALVES, mean_branch, rstd_attn[:, :])
                branch_part(c, 1, 1, False)
                branch_part(c, 2, 1, False)
                statistic(c, ST_CONV, square_added, c * SQUARES + Q_FFN, mean_branch, square_sum[:, :])
                for d in range(KD):
                    if d >= 3:
                        branch_part(c, d, 1, False)
                    branch_part(c, d, 0, True)
                for n in range(4):
                    projection(c, T_UP_A + n, unit(U_UP_A + n), U_UP_A + n, u_hi, u_lo,
                               first=(h_split, c * KD) if n == 0 else None,
                               middle=None if n != 1 else lambda: statistic(
                                   c, ST_FFN, square_added, c * SQUARES + SQUARES, mean_model, square_sum[:, :]))
                up_projection(c, T_UP_A, U_UP_A, PART_A, start=1)
                down_projection(c, T_DOWN_A, U_DOWN_A, PART_A, 0)
                up_projection(c, T_UP_B, U_UP_B, PART_B)
                nxt = c + 1
                down_projection(c, T_DOWN_B, U_DOWN_B, PART_B, PART_A,
                                None if last else lambda: statistic(nxt, ST_MIX, square_added,
                                                                    nxt * SQUARES + Q_CONV, mean_model,
                                                                    square_sum[:, :]))

            pe.wait_ge(consts, 2)
            pe.wait_ge(vec_loaded, 64)
            pe.wait_ge(wide_ready, 1)
            for heads_of in (range(4, 8), range(4)):
                for n in heads_of:
                    mm = pe.matmul(psum[:, n, 0:REL], table_wide[:, n, :], buckets, start=True, stop=True)
                mm.then_inc(rows_done, 1)
            pe.wait_ge(last_rows_copied, 1)
            statistic(0, ST_MIX, square_added, Q_CONV, mean_model, square_sum[:, :])
            pe.wait_ge(first_rows_copied, 1)
            with pe.Fori(0, CHUNKS - 1) as c:
                chunk(c, False)
            chunk(CHUNKS - 1, True)

        @block.scalar
        def _(act):
            state = [0]

            def split_to(c, n):
                while state[0] < n:
                    u = state[0]
                    before = unit_end(u - SLOTS) if u >= SLOTS else unit_end(u - SLOTS + UNITS) - EVENTS
                    split_one(u, c * (UNITS // RAW_SLOTS) * 16 + 16 * (u // RAW_SLOTS + 1),
                              c * EVENTS + (before + 1))
                    state[0] += 1

            def split_one(name, loads, used):
                slot, raw = name % SLOTS, name % RAW_SLOTS
                act.wait_ge(w_loaded[raw], loads)
                if used is not None:
                    act.wait_ge(pe_done, used)
                act.activation(w_hi[:, slot, :], w_raw[:, raw, :], ACT.Copy).then_inc(w_hi_done, 1)

            def root_of(c, index, used, into=rstd, scale=1.0):
                act.wait_ge(stat_done, c * STATS + (index + 1))
                if used is not None:
                    act.wait_ge(*used)
                act.activation(into[:, :], psum[:, STAT_BANK, :], ACT.Ln, bias=eps[:, :], scale=scale) \
                   .then_inc(stat_read, 1)
                act.drain()
                act.activation(into[:, :], into[:, :], ACT.Exp, scale=-0.5).then_inc(rstd_ready, 1)

            def round_tile(c, n, target):
                act.wait_ge(normed_ready, c * NORMED + (n + 1))
                act.activation(target, normed[:, n % 2, :], ACT.Copy).then_inc(hi_done, 1)

            def done(c, tile):
                act.wait_ge(pe_done, c * EVENTS + (tile_end(tile) + 1))

            def load_x(c):
                act.dma_start(x_in[:, :, :], x[bass.ds(c, 1), :, :].rearrange("a p (k t) -> p (a k) t", k=KD)) \
                   .then_inc(x_loaded, 16)

            def qk_square_of(c, n, tile):
                done(c, tile)
                act.activation(square[:, 0, :], psum[:, bank_of(tile), :], ACT.Square).then_inc(qk_square, 1)

            def exps(c, m):
                hf = m % 2
                act.wait_ge(top_ready, c * HALVES + (m + 1))
                for n in range(4):
                    at = 4 * hf + n
                    act.activation(scores[:, m % 2, n, :], scores[:, m % 2, n, :], ACT.Exp, bias=neg_top[:, at:at + 1],
                                   accum_out=denom[:, m // 2 % 2, at:at + 1])
                act.wait_ge(sink_ready, c * HALVES + (m + 1))
                act.activation(sink_exp[:, m // 2 % 2, 4 * hf:4 * hf + 4], sink_less[:, 4 * hf:4 * hf + 4], ACT.Exp) \
                   .then_inc(exp_done, 1)

            def divide(c, m):
                act.wait_ge(share_ready, c * HALVES + (m + 1))
                for n in range(DVE_HEADS, 4):
                    at = 4 * (m % 2) + n
                    share = act.activation(scores[:, m % 2, n, :], scores[:, m % 2, n, :], ACT.Copy,
                                           scale=denom[:, m // 2 % 2, at:at + 1])
                share.then_inc(probs_shared, 1)

            def attention_step(c, m):
                if 1 <= m < HALVES + 1:
                    divide(c, m - 1)
                if m >= 3:
                    half = m - 3
                    i, hf = half // 2, half % 2
                    act.wait_ge(pv_done, c * HALVES + (half + 1))
                    o = psum[:, STAT_BANK, 0:2 * P]
                    for n in range(2):
                        p = 2 * hf + n
                        act.activation(g_hi[:, KD + p, i * P:(i + 1) * P], o[:, n * P:(n + 1) * P], ACT.Copy,
                                       scale=vec[:, V_ATTN_G + p:V_ATTN_G + p + 1])
                    if half:
                        act.wait_ge(heads_summed, c * HALVES + half)
                    act.activation(head_square[:, :, :].rearrange("p n q -> p (n q)"), o, ACT.Square) \
                       .then_inc(heads_squared, 1)
                if 2 <= m < HALVES + 2:
                    for e in range(2):
                        act.wait_ge(turned, c * 2 * HALVES + (2 * (m - 2) + e + 1))
                        act.activation(probs_hi[:, e, :], psum[:, PT_BANKS[e], :], ACT.Copy).then_inc(probs_hi_done, 1)
                if m < HALVES:
                    exps(c, m)

            def conv_step(c, n):
                j, kind = n // 3, n % 3
                if kind == 0:
                    done(c, U_CONV + n)
                    if j >= 1:
                        act.wait_ge(gated_ready, c * CT + j)
                    act.activation(gate_c, psum[:, bank_of(U_CONV + n), :], ACT.Copy).then_inc(c_copied, 1)
                if kind == 1:
                    act.wait_ge(gated_ready, c * CT + (j + 1))
                    if j >= 1:
                        act.wait_ge(y_ready, c * CT + j)
                    w = V_CONV_W + 3 * j + 2
                    act.activation(conv, gated[:, j, 2:2 + T], ACT.Copy, scale=vec[:, w:w + 1]).then_inc(tap_done, 1)

            def y_rounded(c, j):
                act.wait_ge(y_ready, c * CT + (j + 1))
                act.activation(g_hi[:, j, :], normed[:, j % 2, :], ACT.Copy,
                               scale=vec[:, V_CONV_G + j:V_CONV_G + j + 1]).then_inc(y_hi_done, 1)
                square_tile(c, Q_CONV + j, normed[:, j % 2, :])

            def up_phase(c, tile0, unit0, part, f0):
                with act.Fori(0, part // 2) as i:
                    for e in range(2):
                        pair = c * FT + i * 2 + (f0 + e)
                        for gv in range(2):
                            n = 2 * e + gv
                            split_one(unit0 + n + 3, c * (UNITS // RAW_SLOTS * 16) + i * (4 // RAW_SLOTS * 16)
                                      + ((unit0 + n + 3) // RAW_SLOTS + 1) * 16,
                                      c * EVENTS + i * 4 + (tile_end(tile0 + n)))
                        act.wait_ge(gate_ready, pair + 1)
                        act.activation(up_conv[:, 0, :], up_conv[:, 0, :], ACT.Silu).then_inc(silu_done, 1)
                        act.wait_ge(product_ready, pair + 1)
                        act.activation(g_hi[:, bass.ds(i * 2 + e, 1), :].rearrange("p a t -> p (a t)"),
                                       product32, ACT.Copy).then_inc(g_hi_done, 1)
                state[0] += 2 * part

            def chunk(c, last):
                state[0] = 3
                split_to(c, 4)
                qk_square_of(c, 0, U_K)
                split_to(c, 5)
                done(c, U_V)
                act.wait_ge(tails_moved, c + 1)
                act.activation(v_t, psum[:, bank_of(U_V), :], ACT.Copy).then_inc(v_copied, 1)
                root_of(c, ST_K, (normed_ready, c * NORMED + N_K))
                round_tile(c, N_K, k_hi[:, P:P + T])
                split_to(c, 6)
                qk_square_of(c, 1, U_Q)
                act.wait_ge(v_turned, c + 1)
                for e in range(2):
                    own = slice(e * HEAD_DIM, (e + 1) * HEAD_DIM)
                    act.activation(v_hi[:, :, e, own],
                                   psum[:, PT_BANKS[0], :].rearrange("p (b d) -> p b d", b=BLOCKS)[:, :, own],
                                   ACT.Copy).then_inc(v_hi_done, 1)
                for p in range(QT):
                    split_to(c, 7 + p)
                    root_of(c, ST_Q + p, (normed_ready, c * NORMED + N_Q + p))
                    round_tile(c, N_Q + p, g_hi[:, KD + p, :])
                    if p + 1 < QT:
                        qk_square_of(c, 2 + p, U_Q + p + 1)
                conv_step(c, 0)
                for m in range(3 * CT - 1):
                    conv_step(c, 1 + m)
                    if m == 3 * CT - 2:
                        attention_step(c, m)
                    if (1 + m) % 3 == 2:
                        y_rounded(c, (1 + m) // 3)
                    split_to(c, U_CONV + 1 + m + 4)
                    if m < 3 * CT - 2:
                        attention_step(c, m)
                root_of(c, ST_ATTN, None, rstd_attn)
                root_of(c, ST_CONV, (normed_ready, c * NORMED + NORMED))
                for d in range(KD):
                    split_to(c, U_OUT + d + 4)
                    act.wait_ge(h_ready, c * KD + (d + 1))
                    gain = vec[:, V_FFN_G + d:V_FFN_G + d + 1]
                    act.activation(u_hi[:, d, :], h[:, d, :], ACT.Copy, scale=gain).then_inc(h_hi_done, 1)
                    square_tile(c, Q_FFN + d, h[:, d, :])
                if not last:
                    load_x(c + 1)
                root_of(c, ST_FFN, None)
                act.preload_act_table_set(SILU_SET)
                up_phase(c, T_UP_A, U_UP_A, PART_A, 0)
                for d in range(KD):
                    split_to(c, U_DOWN_A + (d * PART_A) // 8 + 4)
                    done(c, T_DOWN_A + d)
                split_to(c, U_UP_B + 3)
                up_phase(c, T_UP_B, U_UP_B, PART_B, PART_A)
                act.preload_act_table_set(LN_EXP_SET)
                split_to(c, U_DOWN_B + 3)
                if not last:
                    norm_mix_with_splits(c)
                for d in range(KD):
                    split_to(c, min(U_DOWN_B + (d * PART_B) // 8 + 4, UNITS if last else UNITS + 3))
                    if d % 4 == 3:
                        act.wait_ge(out_ready, c * KD + (d + 1))
                        lo = d - 3
                        act.dma_start(out[bass.ds(c, 1), :, lo * T:(lo + 4) * T].rearrange("a p n -> p (a n)"),
                                      h[:, lo:lo + 4, :].rearrange("p k t -> p (k t)")).then_inc(out_stored, 16)
                if not last:
                    split_to(c, UNITS + 3)

            def square_tile(c, n, tile):
                if not (isinstance(c, int) and c == 0 and n < 2):
                    act.wait_ge(square_added, c * SQUARES + (n - 1))
                act.activation(square[:, n % 2, :], tile, ACT.Square).then_inc(square_ready, 1)

            def norm_mix_with_splits(c):
                nxt = c + 1
                act.wait_ge(x_loaded, nxt * 16)
                for k in range(KD):
                    square_tile(nxt, Q_MIX + k, x_in[:, k, :])
                split_to(c, U_DOWN_B + 6)
                root_of(nxt, ST_MIX, (g_ready, nxt * FT))
                for k in range(KD):
                    if k % 2 == 0:
                        split_to(c, U_DOWN_B + -(-(3 + k // 2) * PART_B // 8) + 2)
                    round_tile(nxt, N_MIX + k, u_hi[:, k, :])

            act.preload_act_table_set(LN_EXP_SET)
            act.wait_ge(consts, 2)
            for k in range(KD):
                if k % (KD // 2) == 0:
                    act.wait_ge(first_loaded[k // (KD // 2)], 16)
                square_tile(0, Q_MIX + k, x_in[:, k, :])
                if k == KD - 3:
                    act.wait_ge(rows_done, 1)
                    act.activation(rows[:, 4:8, :], psum[:, 4:8, 0:REL], ACT.Copy).then_inc(last_rows_copied, 1)
            split_one(0, 16, None)
            root_of(0, ST_MIX, None)
            for k in range(KD):
                round_tile(0, N_MIX + k, u_hi[:, k, :])
                if k in (1, 5):
                    u = 1 + k // 4
                    split_one(u, 16 * (u // RAW_SLOTS + 1), None)
            with act.Fori(0, CHUNKS - 1) as c:
                chunk(c, False)
            chunk(CHUNKS - 1, True)
            act.wait_ge(out_stored, CHUNKS * 2 * 16 + 1)

        @block.vector
        def _(dve):
            def add_squares(c, first, n):
                for t in range(n):
                    dve.wait_ge(square_ready, c * SQUARES + (first + t + 1))
                    add_square(first + t, t)

            def add_square(n, t):
                if t == 0:
                    dve.tensor_copy(square_sum[:, :], square[:, n % 2, :]).then_inc(square_added, 1)
                else:
                    dve.tensor_tensor(square_sum[:, :], square_sum[:, :], square[:, n % 2, :], ALU.add) \
                       .then_inc(square_added, 1)
                dve.drain()

            def scale_tile(c, n, tile, gain):
                return dve.scalar_tensor_tensor(normed[:, n % 2, :], tile, vec[:, gain:gain + 1], rstd[:, :],
                                                ALU.mult, ALU.mult).then_inc(normed_ready, 1)

            def rest_of(c, n, hi, lo):
                dve.wait_ge(hi_done, c * NORMED + (n + 1))
                dve.tensor_tensor(lo, normed[:, n % 2, :], hi.bitcast(F32), ALU.subtract).then_inc(lo_done, 1)

            def normalise(c, first, tiles, gain0, his, los):
                for t, tile in enumerate(tiles):
                    scale_tile(c, first + t, tile, gain0 + t)
                    if t >= 1:
                        rest_of(c, first + t - 1, his[t - 1], los[t - 1])
                        dve.drain()
                rest_of(c, first + len(tiles) - 1, his[-1], los[-1])
                dve.drain()

            def norm_mix(c):
                dve.wait_ge(rstd_ready, c * STATS + (ST_MIX + 1))
                normalise(c, N_MIX, [x_in[:, k, :] for k in range(KD)], V_MIX_G,
                          [u_hi[:, k, :] for k in range(KD)], [u_lo[:, k, :] for k in range(KD)])

            def norm_mix_beside_down(c):
                nxt = c + 1
                add_squares(nxt, Q_MIX, KD)
                for d in range(3):
                    add_to_h(c, T_DOWN_B, d, out_ready)
                dve.wait_ge(rstd_ready, nxt * STATS + (ST_MIX + 1))
                for d in range(3, KD):
                    ks = range(2 * (d - 3), min(2 * (d - 2), KD))
                    if ks:
                        normalise(nxt, N_MIX + ks[0], [x_in[:, k, :] for k in ks], V_MIX_G + ks[0],
                                  [u_hi[:, k, :] for k in ks], [u_lo[:, k, :] for k in ks])
                    add_to_h(c, T_DOWN_B, d, out_ready)

            def norm_qk(c, n, tile, gain, hi, lo):
                dve.wait_ge(rstd_ready, c * STATS + (ST_K + n + 1))
                scale_tile(c, N_K + n, psum[:, bank_of(tile), :], gain)
                dve.drain()
                dve.sem_inc(bank_free[bank_of(tile)], 1)
                rest_of(c, N_K + n, hi, lo)
                dve.drain()

            def softmax(c, m):
                hf = m % 2
                at = slice(4 * hf, 4 * hf + 4)
                dve.wait_ge(scores_done, c * HALVES + (m + 1))
                if m == 0:
                    dve.wait_ge(bias_loaded, 16)
                    dve.wait_ge(out_stored, c * 32 + 1)
                logits = scores[:, m % 2, :, :]
                dve.scalar_tensor_tensor(logits.rearrange("p n k -> p (n k)"),
                                         psum[:, S_BANK:S_BANK + 2, :].rearrange("p n k -> p (n k)"),
                                         HEAD_DIM ** -0.5, bias[:, at, :].rearrange("p n k -> p (n k)"),
                                         ALU.mult, ALU.add).then_inc(scores_read, 1)
                dve.drain()
                if m < 2:
                    dve.tensor_scalar(logits[:, :, 0:P], logits[:, :, 0:P], edge[:, :], None, ALU.add)
                    dve.drain()
                dve.tensor_reduce(top[:, at], logits, AXIS_X, ALU.max)
                dve.drain()
                sinks = vec[:, V_SINKS + 4 * hf:V_SINKS + 4 * hf + 4]
                dve.scalar_tensor_tensor(neg_top[:, at], top[:, at], -1.0, neg_sinks[:, at], ALU.mult, ALU.min) \
                   .then_inc(top_ready, 1)
                dve.drain()
                dve.tensor_tensor(sink_less[:, at], sinks, neg_top[:, at], ALU.add).then_inc(sink_ready, 1)
                if m == 1:
                    dve.memset(edge[:, :], 0.0)

            def divide(c, m):
                dve.wait_ge(exp_done, c * HALVES + (m + 1))
                hf = m % 2
                total = denom[:, m // 2 % 2, 4 * hf:4 * hf + 4]
                dve.tensor_tensor(total, total, sink_exp[:, m // 2 % 2, 4 * hf:4 * hf + 4], ALU.add)
                dve.drain()
                dve.reciprocal(total, total).then_inc(share_ready, 1)
                dve.drain()
                dve.tensor_tensor(scores[:, m % 2, 0:DVE_HEADS, :], scores[:, m % 2, 0:DVE_HEADS, :],
                                  total[:, 0:DVE_HEADS].rearrange("p (n o) -> p n o", o=1)
                                  .broadcast_to([P, DVE_HEADS, 2 * P]), ALU.mult).then_inc(probs_ready, 1)

            def split_heads(c, half):
                i, hf = half // 2, half % 2
                dve.wait_ge(heads_squared, c * HALVES + (half + 1))
                for n in range(2):
                    p = 2 * hf + n
                    lo = dve.scalar_tensor_tensor(g_lo[:, KD + p, i * P:(i + 1) * P],
                                                  psum[:, STAT_BANK, n * P:(n + 1) * P],
                                                  vec[:, V_ATTN_G + p:V_ATTN_G + p + 1],
                                                  g_hi[:, KD + p, i * P:(i + 1) * P].bitcast(F32),
                                                  ALU.mult, ALU.subtract)
                lo.then_inc(attn_split, 1)

            def sum_head_squares(c, half):
                i, hf = half // 2, half % 2
                total = rstd_attn[:, i * P:(i + 1) * P]
                if hf == 0:
                    dve.tensor_tensor(total, head_square[:, 0, :], head_square[:, 1, :], ALU.add) \
                       .then_inc(heads_summed, 1)
                else:
                    dve.tensor_tensor(total, total, head_square[:, 0, :], ALU.add)
                    dve.drain()
                    dve.tensor_tensor(total, total, head_square[:, 1, :], ALU.add).then_inc(heads_summed, 1)

            def split_probs(c, m):
                for e in range(2):
                    dve.wait_ge(probs_hi_done, c * 2 * HALVES + (2 * m + e + 1))
                    lo = dve.tensor_tensor(probs_lo[:, e, :], psum[:, PT_BANKS[e], :], probs_hi[:, e, :].bitcast(F32),
                                           ALU.subtract)
                lo.then_inc(probs_split, 1)

            def copied_c(c, j, tile):
                dve.wait_ge(c_copied, c * CT + (j + 1))
                dve.sem_inc(bank_free[bank_of(tile)], 1)

            def conv_taps(c, j):
                dve.wait_ge(tap_done, c * CT + (j + 1))
                for k in (1, 0):
                    w = V_CONV_W + 3 * j + k
                    dve.scalar_tensor_tensor(conv, gated[:, j, k:k + T], vec[:, w:w + 1], conv, ALU.mult, ALU.add)
                    dve.drain()
                dve.tensor_copy(gated[:, j, 0:2], gated[:, j, T:T + 2])

            def up_tile(done, n, f):
                gv = n % 2
                dve.wait_ge(pe_done, done)
                dve.tensor_tensor(up[:, gv, 2:2 + T], psum[:, n, :], rstd[:, :], ALU.mult).then_inc(bank_free[n], 1)
                tail = up_tail[:, bass.ds(f, 1), gv, :].rearrange("p a t -> p (a t)")
                dve.tensor_copy(up[:, gv, 0:2], tail)
                dve.drain()
                w = [vec[:, bass.ds(f * 8 + (V_FFN + gv * 4 + k), 1)] for k in range(4)]
                dve.tensor_scalar(up_conv[:, gv, :], up[:, gv, 2:2 + T], w[2], w[3], ALU.mult, ALU.add)
                dve.tensor_copy(tail, up[:, gv, T:T + 2])
                dve.drain()
                dve.scalar_tensor_tensor(up_conv[:, gv, :], up[:, gv, 1:1 + T], w[1], up_conv[:, gv, :],
                                         ALU.mult, ALU.add)
                dve.drain()
                return dve.scalar_tensor_tensor(up_conv[:, gv, :], up[:, gv, 0:T], w[0], up_conv[:, gv, :],
                                                ALU.mult, ALU.add)

            def up_phase(c, tile0, part, f0):
                with dve.Fori(0, part // 2) as i:
                    for e in range(2):
                        f = i * 2 + (f0 + e)
                        pair = c * FT + f
                        n = 2 * e
                        if tile0 == T_UP_A and e == 0:
                            dve.wait_ge(rstd_ready, c * STATS + (ST_FFN + 1))
                        up_tile(c * EVENTS + i * 4 + (tile_end(tile0 + n) + 1), n, f).then_inc(gate_ready, 1)
                        up_tile(c * EVENTS + i * 4 + (tile_end(tile0 + n + 1) + 1), n + 1, f)
                        dve.drain()
                        dve.wait_ge(silu_done, pair + 1)
                        dve.tensor_tensor(product32, up_conv[:, 0, :], up_conv[:, 1, :], ALU.mult) \
                           .then_inc(product_ready, 1)
                        dve.wait_ge(g_hi_done, pair + 1)
                        gh, gl = (g[:, bass.ds(i * 2 + e, 1), :].rearrange("p a t -> p (a t)") for g in (g_hi, g_lo))
                        dve.tensor_tensor(gl, product32, gh.bitcast(F32), ALU.subtract).then_inc(g_ready, 1)
                        dve.drain()

            def add_to_h(c, tile0, d, ready=None):
                dve.wait_ge(pe_done, c * EVENTS + (tile_end(tile0 + d) + 1))
                bank = bank_of(tile0 + d)
                dve.tensor_tensor(h[:, d, :], psum[:, bank, :], h[:, d, :], ALU.add).then_inc(bank_free[bank], 1)
                dve.drain()
                if ready is not None:
                    dve.sem_inc(ready, 1)

            def out_tile(c, d):
                dve.wait_ge(pe_done, c * EVENTS + (tile_end(T_OUT + d) + 1))
                part = normed[:, d % 2, :]
                banks = [bank_of(T_OUT + d, n) for n in range(2)]
                dve.tensor_tensor(part, psum[:, banks[0], :], rstd[:, :], ALU.mult).then_inc(bank_free[banks[0]], 1)
                dve.tensor_tensor(h[:, d, :], psum[:, banks[1], :], rstd_attn[:, :], ALU.mult) \
                   .then_inc(bank_free[banks[1]], 1)
                dve.drain()
                dve.tensor_tensor(part, part, x_in[:, d, :], ALU.add)
                dve.drain()
                dve.tensor_tensor(h[:, d, :], h[:, d, :], part, ALU.add).then_inc(h_ready, 1)

            def split_h(c, d):
                dve.wait_ge(h_hi_done, c * KD + (d + 1))
                gain = vec[:, V_FFN_G + d:V_FFN_G + d + 1]
                dve.scalar_tensor_tensor(u_lo[:, d, :], h[:, d, :], gain, u_hi[:, d, :].bitcast(F32),
                                         ALU.mult, ALU.subtract).then_inc(h_split, 1)
                dve.wait_ge(square_ready, c * SQUARES + (Q_FFN + d + 1))
                add_square(Q_FFN + d, d)

            def chunk(c, last):
                for k in (k_hi, k_lo):
                    dve.tensor_copy(k[:, 0:P], k[:, T:T + P].bitcast(F32))
                dve.drain()
                dve.sem_inc(tails_moved, 1)
                dve.wait_ge(v_copied, c + 1)
                dve.sem_inc(bank_free[bank_of(U_V)], 1)
                norm_qk(c, 0, U_K, V_K_G, k_hi[:, P:P + T], k_lo[:, P:P + T])
                for e in range(2):
                    own, other = (slice(a * HEAD_DIM, (a + 1) * HEAD_DIM) for a in (e, 1 - e))
                    for v in (v_hi, v_lo):
                        dve.memset(v[:, :, e, other].bitcast(F32), 0.0)
                    dve.wait_ge(v_hi_done, c * 2 + 2)
                    lo = dve.tensor_tensor(v_lo[:, :, e, own],
                                           psum[:, PT_BANKS[0], :].rearrange("p (b d) -> p b d", b=BLOCKS)[:, :, own],
                                           v_hi[:, :, e, own].bitcast(F32), ALU.subtract)
                lo.then_inc(v_split, 1)
                for p in range(QT):
                    norm_qk(c, 1 + p, U_Q + p, V_Q_G, g_hi[:, KD + p, :], g_lo[:, KD + p, :])
                for m in range(-1, 3 * CT - 1):
                    n = m + 1
                    j, kind = n // 3, n % 3
                    tile = U_CONV + n
                    if kind == 1:
                        dve.wait_ge(pe_done, c * EVENTS + (tile_end(tile) + 1))
                        dve.tensor_tensor(gated[:, j, 2:2 + T], psum[:, bank_of(tile), :], gate_c, ALU.mult) \
                           .then_inc(gated_ready, 1)
                        dve.drain()
                        dve.sem_inc(bank_free[bank_of(tile)], 1)
                    if m == 3 * CT - 2:
                        split_heads(c, m - 3)
                        sum_head_squares(c, m - 3)
                    if kind == 2:
                        dve.wait_ge(pe_done, c * EVENTS + (tile_end(tile) + 1))
                        dve.tensor_tensor(normed[:, j % 2, :], psum[:, bank_of(tile), :], conv, ALU.mult) \
                           .then_inc(y_ready, 1)
                        dve.drain()
                        dve.sem_inc(bank_free[bank_of(tile)], 1)
                    if m < 0:
                        copied_c(c, j, tile)
                        continue
                    if 1 <= m < HALVES + 1:
                        divide(c, m - 1)
                    if m < 2:
                        softmax(c, m)
                    if kind == 1:
                        conv_taps(c, j)
                    if kind == 2:
                        dve.wait_ge(y_hi_done, c * CT + (j + 1))
                        gain = vec[:, V_CONV_G + j:V_CONV_G + j + 1]
                        dve.scalar_tensor_tensor(g_lo[:, j, :], normed[:, j % 2, :], gain,
                                                 g_hi[:, j, :].bitcast(F32), ALU.mult, ALU.subtract) \
                           .then_inc(conv_split, 1)
                        dve.wait_ge(square_ready, c * SQUARES + (Q_CONV + j + 1))
                        add_square(Q_CONV + j, j)
                    if 2 <= m < HALVES:
                        softmax(c, m)
                    if kind == 0:
                        copied_c(c, j, tile)
                    if 3 <= m < 3 * CT - 2:
                        split_heads(c, m - 3)
                        sum_head_squares(c, m - 3)
                    if 2 <= m < HALVES + 2:
                        split_probs(c, m - 2)
                if not last:
                    for before, v in ((v_before_hi, v_hi), (v_before_lo, v_lo)):
                        dve.tensor_copy(before[:, 0, :, :], v[:, BLOCKS - 1, :, :].bitcast(F32))
                dve.wait_ge(rstd_ready, c * STATS + (ST_CONV + 1))
                for d in range(KD):
                    out_tile(c, d)
                    if d >= 1:
                        split_h(c, d - 1)
                split_h(c, KD - 1)
                up_phase(c, T_UP_A, PART_A, 0)
                for d in range(KD):
                    add_to_h(c, T_DOWN_A, d)
                up_phase(c, T_UP_B, PART_B, PART_A)
                if last:
                    for d in range(KD):
                        add_to_h(c, T_DOWN_B, d, out_ready)
                else:
                    norm_mix_beside_down(c)

            dve.memset(mean_model, 1.0 / D_MODEL)
            dve.memset(mean_branch, 1.0 / CONV_WIDTH)
            dve.memset(edge[:, :], MASKED)
            dve.memset(eps[:, :], EPS)
            dve.memset(k_hi[:, T:T + P].bitcast(F32), 0.0)
            dve.memset(k_lo[:, T:T + P].bitcast(F32), 0.0)
            dve.memset(v_before_hi[:, :, :, :].bitcast(F32), 0.0)
            dve.memset(v_before_lo[:, :, :, :].bitcast(F32), 0.0)
            dve.memset(up_tail[:, :, :, :], 0.0)
            dve.memset(gated[:, :, 0:2], 0.0)
            dve.drain()
            dve.sem_inc(pe_done, 1)
            dve.sem_inc(out_stored, 1)
            for b in range(BANKS):
                dve.sem_inc(bank_free[b], 1)
            dve.sem_inc(consts, 2)
            dve.wait_ge(vec_loaded, 64)
            dve.memset(table[NUM_BUCKETS:NUM_BUCKETS + 1, :], 1.0)
            dve.tensor_scalar(neg_sinks[:, :], vec[:, V_SINKS:V_SINKS + N_HEADS], -1.0, None, ALU.mult)
            dve.drain()
            dve.tensor_copy(table_wide, table[:, :].rearrange("p (n o) -> p n o", o=1)
                            .broadcast_to([NUM_BUCKETS + 1, N_HEADS, P])).then_inc(wide_ready, 1)
            add_squares(0, Q_MIX, KD)
            dve.wait_ge(rows_done, 2)
            dve.tensor_copy(rows[:, 0:4, :], psum[:, 0:4, 0:REL]).then_inc(first_rows_copied, 1)
            norm_mix(0)
            with dve.Fori(0, CHUNKS - 1) as c:
                chunk(c, False)
            chunk(CHUNKS - 1, True)


def relative_buckets():
    a = np.zeros((NUM_BUCKETS + 1, REL), np.float32)
    for m in range(REL):
        d = 2 * P - 1 - m
        if 0 <= d < WINDOW:
            b = d
            if d >= MAX_EXACT:
                b = MAX_EXACT + int(math.log(d / MAX_EXACT) / math.log(MAX_DISTANCE / MAX_EXACT)
                                    * (NUM_BUCKETS - MAX_EXACT))
            a[min(b, NUM_BUCKETS - 1), m] = 1.0
        else:
            a[NUM_BUCKETS, m] = MASKED
    return a


def lay_out(a):
    a = {k: np.asarray(v) for k, v in a.items()}
    pairs = [n for p in range(QT) for n in (p, p + QT)]
    scored = [2 * f + n + QT * e for f in range(2) for e in range(2) for n in range(2)]
    x = a["x"][0].reshape(CHUNKS, T, KD, P).transpose(0, 3, 2, 1).reshape(CHUNKS, P, KD * T)

    def units(w, order):
        k, n = w.shape
        return w.reshape(k // P, P, n // P, P).transpose(2, 1, 0, 3)[order].reshape(len(order), P, k)

    w_in = a["w_in"][0]
    q0 = 3 * CONV_WIDTH
    q = w_in[:, q0:q0 + ATTN_WIDTH].reshape(D_MODEL, N_HEADS, HEAD_DIM)[:, pairs].reshape(D_MODEL, ATTN_WIDTH)
    w_in = np.concatenate([w_in[:, :q0], q, w_in[:, q0 + ATTN_WIDTH:]], axis=1)
    first = 3 * CT + QT
    order = [first, first + 1] + [3 * CT + p for p in range(QT)]
    for j in range(CT):
        order += [CT + j, 2 * CT + j, j]
    w_out = a["w_out"][0]
    w_attn = w_out[CONV_WIDTH:].reshape(N_HEADS, HEAD_DIM, D_MODEL)[pairs].reshape(ATTN_WIDTH, D_MODEL)
    w_out = np.concatenate([w_out[:CONV_WIDTH], w_attn])
    w_up, w_down = a["w_up"][0], a["w_down"][0]

    def up(f0, n):
        return units(w_up, [g * FT + f for f in range(f0, f0 + n) for g in range(2)])

    def down(f0, n):
        w = w_down.reshape(FT, P, KD, P)[f0:f0 + n].transpose(2, 0, 1, 3).reshape(n * KD // 8, 8, P, P)
        return w.transpose(0, 2, 1, 3).reshape(n * KD // 8, P, 8 * P)

    weights = np.concatenate([units(w_in, order), units(w_out, list(range(KD))),
                              up(0, PART_A), down(0, PART_A), up(PART_A, PART_B), down(PART_A, PART_B)])

    def columns(v):
        return v.reshape(-1, P).T

    conv = a["conv_w"][0].reshape(3, CT, P).transpose(2, 1, 0).reshape(P, 3 * CT)
    taps = np.concatenate([a["ffn_conv_w"][0], a["ffn_conv_b"]]).reshape(4, 2, FT, P)
    attn_g = a["out_norm_attn_g"][0].reshape(N_HEADS, HEAD_DIM)[pairs].reshape(-1)
    vectors = np.concatenate([
        columns(a["norm_mix_g"][0]), columns(a["norm_ffn_g"][0]), columns(a["out_norm_conv_g"][0]), columns(attn_g),
        columns(np.tile(a["q_norm_g"][0], 2)), columns(np.tile(a["k_norm_g"][0], 2)), conv,
        np.broadcast_to(a["sinks"][0][scored], (P, N_HEADS)),
        taps.transpose(3, 2, 1, 0).reshape(P, FT * 8)], axis=1)
    same_head = np.kron(np.eye(2), np.ones((HEAD_DIM, HEAD_DIM))) / HEAD_DIM
    fixed = np.concatenate([np.eye(P), same_head], axis=1).astype(np.float32)
    out = {"x": x, "weights": weights, "vectors": vectors, "rel_table": a["rel_bias_table"][:, scored],
           "fixed": fixed, "bucket_rows": relative_buckets()}
    return {k: np.ascontiguousarray(v) for k, v in out.items()}


def kernel(**inputs):
    import concourse.bacc as bacc
    from concourse.bass_utils import run_bass_kernel_spmd

    nc = bacc.Bacc("TRN2", target_bir_lowering=False, num_devices=1)
    arrays = lay_out(inputs)
    args = [nc.dram_tensor(n, a.shape, F32, kind="ExternalInput").ap() for n, a in arrays.items()]
    bias_rows = nc.dram_tensor("bias_rows", (N_HEADS, P, REL), F32, kind="Internal").ap()
    out = nc.dram_tensor("out", (CHUNKS, P, KD * T), F32, kind="ExternalOutput").ap()
    build_layer(nc, *args, bias_rows, out)
    result = run_bass_kernel_spmd(nc, [arrays], core_ids=[0]).results[0]["out"]
    return result.reshape(CHUNKS, P, KD, T).transpose(0, 3, 2, 1).reshape(1, SEQ, D_MODEL)
```
